# Optimizing a Trainium2 kernel written in Bass

```python
import math
import jax
import jax.numpy as jnp
from jax import lax
import numpy as np

D_MODEL = 1024
BATCH = 1
SEQ = 256
DEPTH = 2

MEM_LEN = 256
ROPE_THETA = 500000.0
ROPE_FRAC = 4
LN_EPS = 1e-5
NEG_INF = -1e30
DEEPNORM_ALPHA = (2 * DEPTH) ** 0.25
DEEPNORM_BETA = (8 * DEPTH) ** -0.25

A_HEADS = 4
A_QK_DIM = D_MODEL // 32
A_V_DIM = 2 * A_QK_DIM
A_QBLK = 128
B_HEADS = 6
B_HEAD_DIM = D_MODEL // 16
B_GROUPS = ((128, 1), (512, 4), (2048, 16))
C_HEADS = 4
C_K_DIM = 3 * D_MODEL // 64
C_V_DIM = 3 * D_MODEL // 32
C_GATE_RANK = 16
C_GATE_TAU = 16.0
C_CHUNK = 16

IN_SPLITS = (
    A_HEADS * 2 * A_QK_DIM, A_HEADS * 2 * A_QK_DIM, A_HEADS * A_V_DIM,
    B_HEADS * B_HEAD_DIM, B_HEADS * B_HEAD_DIM, B_HEADS * B_HEAD_DIM,
    C_HEADS * C_K_DIM, C_HEADS * C_K_DIM, C_HEADS * C_V_DIM, C_HEADS * C_V_DIM,
    C_GATE_RANK,
)
IN_BOUNDS = tuple(int(c) for c in np.cumsum((0,) + IN_SPLITS))
IN_COLS = IN_BOUNDS[-1]
VALUE_SLOTS = (2, 5, 8)

XA_HEADS = 4
XA_HEAD_DIM = D_MODEL // XA_HEADS
F_DENSE = ((8 * D_MODEL // 3 + 127) // 128) * 128
N_EXPERTS = 8
TOP_K = 2
F_MOE = 7 * D_MODEL // 2
N_DENSE = (DEPTH + 1) // 2
N_MOE = DEPTH // 2

kernel_name = 'hybrid_diff_dilated_gla_deepnorm_moe'

def layer_norm(x, g, b):
    xf = x.astype(jnp.float32)
    mu = xf.mean(-1, keepdims=True)
    var = jnp.square(xf - mu).mean(-1, keepdims=True)
    return ((xf - mu) * lax.rsqrt(var + LN_EPS) * g + b).astype(x.dtype)

def rms_norm(x, g):
    xf = x.astype(jnp.float32)
    return (xf * lax.rsqrt(jnp.mean(xf * xf, -1, keepdims=True) + LN_EPS) * g).astype(x.dtype)

def apply_partial_rope(x, positions):
    rot = x.shape[-1] // ROPE_FRAC
    inv_freq = ROPE_THETA ** (-jnp.arange(0, rot, 2, dtype=jnp.float32) / rot)
    ang = positions.astype(jnp.float32)[..., None] * inv_freq
    bshape = ang.shape[:2] + (1,) * (x.ndim - 3) + ang.shape[-1:]
    cos = jnp.cos(ang).reshape(bshape).astype(x.dtype)
    sin = jnp.sin(ang).reshape(bshape).astype(x.dtype)
    x1, x2, xp = x[..., :rot // 2], x[..., rot // 2:rot], x[..., rot:]
    return jnp.concatenate([x1 * cos - x2 * sin, x2 * cos + x1 * sin, xp], axis=-1)

def diff_attention(q, k, v, lam, lam_init, norm_g):
    bsz, seq, heads, _, dqk = q.shape
    nqb = seq // A_QBLK
    scale = dqk ** -0.5
    q_blocks = q.reshape(bsz, nqb, A_QBLK, heads, 2, dqk).transpose(1, 0, 2, 3, 4, 5)
    starts = jnp.arange(nqb, dtype=jnp.int32) * A_QBLK
    kpos = jnp.arange(seq, dtype=jnp.int32)

    def one_block(args):
        qb, start = args
        s = jnp.einsum('bqhmd,bkhmd->bhmqk', qb, k, preferred_element_type=jnp.float32) * scale
        qpos = start + jnp.arange(A_QBLK, dtype=jnp.int32)
        causal = kpos[None, :] <= qpos[:, None]
        p = jax.nn.softmax(jnp.where(causal, s, NEG_INF), axis=-1)
        a = p[:, :, 0] - lam * p[:, :, 1]
        return jnp.einsum('bhqk,bkhd->bqhd', a.astype(v.dtype), v)

    o = lax.map(one_block, (q_blocks, starts))
    o = o.transpose(1, 0, 2, 3, 4).reshape(bsz, seq, heads, v.shape[-1])
    return rms_norm(o, norm_g) * (1.0 - lam_init)

def dilated_group(q, k, v, window, dilation):
    bsz, seq, heads, dh = q.shape
    span = window // dilation
    sub_len = seq // dilation
    nb = -(-sub_len // span)
    pad = nb * span - sub_len

    def to_blocks(t):
        t = t.reshape(bsz, sub_len, dilation, heads, dh).transpose(0, 2, 3, 1, 4)
        t = jnp.pad(t, ((0, 0), (0, 0), (0, 0), (0, pad), (0, 0)))
        return t.reshape(bsz, dilation, heads, nb, span, dh)

    def with_prev(t):
        prev = jnp.pad(t, ((0, 0), (0, 0), (0, 0), (1, 0), (0, 0), (0, 0)))[:, :, :, :-1]
        return jnp.concatenate([prev, t], axis=4)

    qb = to_blocks(q)
    kk = with_prev(to_blocks(k))
    vv = with_prev(to_blocks(v))
    s = jnp.einsum('brhnqd,brhnkd->brhnqk', qb, kk, preferred_element_type=jnp.float32) * dh ** -0.5
    qi = jnp.arange(span)[:, None]
    ki = jnp.arange(2 * span)[None, :]
    dist = qi + span - ki
    band = (dist >= 0) & (dist <= span)
    has_prev = (jnp.arange(nb) > 0)[:, None, None] | (ki >= span)[None]
    valid = band[None] & has_prev
    s = jnp.where(valid, s, NEG_INF)
    m = s.max(-1, keepdims=True)
    p = jnp.exp(s - m)
    l = p.sum(-1, keepdims=True)
    o = jnp.einsum('brhnqk,brhnkd->brhnqd', (p / l).astype(v.dtype), vv)
    lse = (m + jnp.log(l))[..., 0]

    def from_blocks(t):
        t = t.reshape((bsz, dilation, heads, nb * span) + t.shape[5:])[:, :, :, :sub_len]
        t = jnp.moveaxis(t, 3, 1)
        return t.reshape((bsz, seq, heads) + t.shape[4:])

    return from_blocks(o), from_blocks(lse)

def dilated_attention(q, k, v):
    outs, lses = zip(*[dilated_group(q, k, v, w, r) for (w, r) in B_GROUPS])
    wts = jax.nn.softmax(jnp.stack(lses, axis=0), axis=0)
    return jnp.einsum('gbsh,gbshd->bshd', wts.astype(q.dtype), jnp.stack(outs, axis=0))

def gla_chunked(q, k, v, log_a):
    bsz, seq, heads, dk = q.shape
    dv = v.shape[-1]
    n = seq // C_CHUNK

    def to_chunks(t):
        return t.astype(jnp.float32).reshape(bsz, n, C_CHUNK, heads, t.shape[-1]).transpose(0, 3, 1, 2, 4)

    q, k, v, log_a = map(to_chunks, (q, k, v, log_a))
    q = q * dk ** -0.5
    b = jnp.cumsum(log_a, axis=3)
    causal = jnp.tril(jnp.ones((C_CHUNK, C_CHUNK), dtype=bool))
    diff = b[:, :, :, :, None, :] - b[:, :, :, None, :, :]
    decay = jnp.exp(jnp.where(causal[:, :, None], diff, NEG_INF))
    scores = jnp.einsum('bhnid,bhnjd,bhnijd->bhnij', q, k, decay)
    o_intra = jnp.einsum('bhnij,bhnjv->bhniv', scores, v)
    b_last = b[:, :, :, -1]
    u = jnp.einsum('bhncd,bhncv->bhndv', k * jnp.exp(b_last[:, :, :, None] - b), v)

    def step(state, inp):
        g, u_n = inp
        return jnp.exp(g)[..., None] * state + u_n, state

    init = jnp.zeros((bsz, heads, dk, dv), jnp.float32)
    _, s_prev = lax.scan(step, init, (jnp.moveaxis(b_last, 2, 0), jnp.moveaxis(u, 2, 0)))
    s_prev = jnp.moveaxis(s_prev, 0, 2)
    o_inter = jnp.einsum('bhncd,bhndv->bhncv', q * jnp.exp(b), s_prev)
    return (o_intra + o_inter).transpose(0, 2, 3, 1, 4).reshape(bsz, seq, heads, dv)

def hybrid_mixer(x, positions, w_in, lam_q1, lam_k1, lam_q2, lam_k2, lam_init,
                 diff_g, gla_wa2, gla_ba, gla_g, w_out):
    bsz, seq, _ = x.shape
    h = x @ w_in
    qa, ka, va, qb, kb, vb, qc, kc, vc, gc, rc = jnp.split(h, IN_BOUNDS[1:-1], axis=-1)
    qa = apply_partial_rope(qa.reshape(bsz, seq, A_HEADS, 2, A_QK_DIM), positions)
    ka = apply_partial_rope(ka.reshape(bsz, seq, A_HEADS, 2, A_QK_DIM), positions)
    va = va.reshape(bsz, seq, A_HEADS, A_V_DIM)
    f32 = jnp.float32
    lam = (jnp.exp(jnp.sum(lam_q1.astype(f32) * lam_k1.astype(f32)))
           - jnp.exp(jnp.sum(lam_q2.astype(f32) * lam_k2.astype(f32))) + lam_init)
    oa = diff_attention(qa, ka, va, lam, lam_init, diff_g)
    qb = apply_partial_rope(qb.reshape(bsz, seq, B_HEADS, B_HEAD_DIM), positions)
    kb = apply_partial_rope(kb.reshape(bsz, seq, B_HEADS, B_HEAD_DIM), positions)
    vb = vb.reshape(bsz, seq, B_HEADS, B_HEAD_DIM)
    ob = dilated_attention(qb, kb, vb)
    log_a = jax.nn.log_sigmoid((rc @ gla_wa2 + gla_ba).astype(f32)) / C_GATE_TAU
    oc = gla_chunked(qc.reshape(bsz, seq, C_HEADS, C_K_DIM), kc.reshape(bsz, seq, C_HEADS, C_K_DIM),
                     vc.reshape(bsz, seq, C_HEADS, C_V_DIM), log_a.reshape(bsz, seq, C_HEADS, C_K_DIM))
    oc = rms_norm(oc, gla_g).astype(x.dtype) * jax.nn.silu(gc.reshape(bsz, seq, C_HEADS, C_V_DIM))
    o = jnp.concatenate([oa.reshape(bsz, seq, -1), ob.reshape(bsz, seq, -1),
                         oc.reshape(bsz, seq, -1)], axis=-1)
    return o @ w_out

def memory_cross_attention(x, mem, wq, wkv, wo):
    bsz, seq, _ = x.shape
    q = (x @ wq).reshape(bsz, seq, XA_HEADS, XA_HEAD_DIM)
    k, v = jnp.split(mem @ wkv, 2, axis=-1)
    k = k.reshape(bsz, mem.shape[1], XA_HEADS, XA_HEAD_DIM)
    v = v.reshape(bsz, mem.shape[1], XA_HEADS, XA_HEAD_DIM)
    s = jnp.einsum('bqhd,bkhd->bhqk', q, k, preferred_element_type=jnp.float32) * XA_HEAD_DIM ** -0.5
    p = jax.nn.softmax(s, axis=-1)
    o = jnp.einsum('bhqk,bkhd->bqhd', p.astype(v.dtype), v).reshape(bsz, seq, D_MODEL)
    return o @ wo

def swiglu(x, w13, w2):
    gate, up = jnp.split(x @ w13, 2, axis=-1)
    return (jax.nn.silu(gate) * up) @ w2

def moe_swiglu(x, router, w13, w2):
    logits = (x @ router).astype(jnp.float32)
    top_vals, top_idx = lax.top_k(logits, TOP_K)
    top_w = jax.nn.softmax(top_vals, axis=-1)
    gates = jnp.einsum('bsk,bske->bse', top_w, jax.nn.one_hot(top_idx, N_EXPERTS, dtype=jnp.float32))
    out = jnp.zeros_like(x)
    for e in range(N_EXPERTS):
        out = out + gates[..., e:e + 1].astype(x.dtype) * swiglu(x, w13[e], w2[e])
    return out

def setup_inputs(seed: int = 0) -> dict:
    key = jax.random.key(seed)
    ks = jax.random.split(key, 28)

    def nrm(k, shape, scale):
        return jax.random.normal(k, shape, jnp.float32) * scale

    def gain(k, shape):
        return 1.0 + 0.02 * jax.random.normal(k, shape, jnp.float32)

    def bias(k, shape):
        return 0.02 * jax.random.normal(k, shape, jnp.float32)

    col_scale = np.ones((IN_COLS,), np.float32)
    for slot in VALUE_SLOTS:
        col_scale[IN_BOUNDS[slot]:IN_BOUNDS[slot + 1]] = DEEPNORM_BETA
    offset = jax.random.randint(ks[2], (BATCH, 1), 0, 4096, dtype=jnp.int32)
    positions = (offset + jnp.arange(SEQ, dtype=jnp.int32)[None, :]).astype(jnp.int32)
    ds = D_MODEL ** -0.5
    return {
        'x': nrm(ks[0], (BATCH, SEQ, D_MODEL), 1.0),
        'mem': nrm(ks[1], (BATCH, MEM_LEN, D_MODEL), 1.0),
        'positions': positions,
        'w_in': nrm(ks[3], (DEPTH, D_MODEL, IN_COLS), ds) * jnp.asarray(col_scale),
        'lam_q1': nrm(ks[4], (DEPTH, A_QK_DIM), 0.1),
        'lam_k1': nrm(ks[5], (DEPTH, A_QK_DIM), 0.1),
        'lam_q2': nrm(ks[6], (DEPTH, A_QK_DIM), 0.1),
        'lam_k2': nrm(ks[7], (DEPTH, A_QK_DIM), 0.1),
        'diff_norm_g': gain(ks[8], (DEPTH, A_V_DIM)),
        'gla_wa2': nrm(ks[9], (DEPTH, C_GATE_RANK, C_HEADS * C_K_DIM), C_GATE_RANK ** -0.5),
        'gla_ba': nrm(ks[10], (DEPTH, C_HEADS * C_K_DIM), 0.1),
        'gla_norm_g': gain(ks[11], (DEPTH, C_V_DIM)),
        'w_out': nrm(ks[12], (DEPTH, D_MODEL, D_MODEL), ds * DEEPNORM_BETA),
        'ln_mix_g': gain(ks[13], (DEPTH, D_MODEL)),
        'ln_mix_b': bias(ks[14], (DEPTH, D_MODEL)),
        'xa_wq': nrm(ks[15], (DEPTH, D_MODEL, D_MODEL), ds),
        'xa_wkv': jnp.concatenate([nrm(ks[16], (DEPTH, D_MODEL, D_MODEL), ds),
                                   nrm(ks[17], (DEPTH, D_MODEL, D_MODEL), ds * DEEPNORM_BETA)], axis=-1),
        'xa_wo': nrm(ks[18], (DEPTH, D_MODEL, D_MODEL), ds * DEEPNORM_BETA),
        'ln_xa_g': gain(ks[19], (DEPTH, D_MODEL)),
        'ln_xa_b': bias(ks[20], (DEPTH, D_MODEL)),
        'ffd_w13': nrm(ks[21], (N_DENSE, D_MODEL, 2 * F_DENSE), ds * DEEPNORM_BETA),
        'ffd_w2': nrm(ks[22], (N_DENSE, F_DENSE, D_MODEL), F_DENSE ** -0.5 * DEEPNORM_BETA),
        'moe_router': nrm(ks[23], (N_MOE, D_MODEL, N_EXPERTS), ds),
        'moe_w13': nrm(ks[24], (N_MOE, N_EXPERTS, D_MODEL, 2 * F_MOE), ds * DEEPNORM_BETA),
        'moe_w2': nrm(ks[25], (N_MOE, N_EXPERTS, F_MOE, D_MODEL), F_MOE ** -0.5 * DEEPNORM_BETA),
        'ln_ffn_g': gain(ks[26], (DEPTH, D_MODEL)),
        'ln_ffn_b': bias(ks[27], (DEPTH, D_MODEL)),
    }

def reference(x, mem, positions, w_in, lam_q1, lam_k1, lam_q2, lam_k2, diff_norm_g, gla_wa2, gla_ba,
              gla_norm_g, w_out, ln_mix_g, ln_mix_b, xa_wq, xa_wkv, xa_wo, ln_xa_g, ln_xa_b,
              ffd_w13, ffd_w2, moe_router, moe_w13, moe_w2, ln_ffn_g, ln_ffn_b):
    for l in range(DEPTH):
        lam_init = 0.8 - 0.6 * math.exp(-0.3 * l)
        mix = hybrid_mixer(x, positions, w_in[l], lam_q1[l], lam_k1[l], lam_q2[l], lam_k2[l], lam_init,
                           diff_norm_g[l], gla_wa2[l], gla_ba[l], gla_norm_g[l], w_out[l])
        x = layer_norm(DEEPNORM_ALPHA * x + mix, ln_mix_g[l], ln_mix_b[l])
        xa = memory_cross_attention(x, mem, xa_wq[l], xa_wkv[l], xa_wo[l])
        x = layer_norm(DEEPNORM_ALPHA * x + xa, ln_xa_g[l], ln_xa_b[l])
        if l % 2 == 0:
            f = swiglu(x, ffd_w13[l // 2], ffd_w2[l // 2])
        else:
            f = moe_swiglu(x, moe_router[l // 2], moe_w13[l // 2], moe_w2[l // 2])
        x = layer_norm(DEEPNORM_ALPHA * x + f, ln_ffn_g[l], ln_ffn_b[l])
    return x


_drawn_inputs = setup_inputs


def setup_inputs(seed=0):
    import zlib

    import numpy as np

    out = dict(_drawn_inputs(seed))
    spreads = {}
    factors = {'lam_q1': 5.85,
     'lam_k1': 2.85,
     'lam_q2': 8.0,
     'lam_k2': 4.877,
     'diff_norm_g': 23.648,
     'gla_wa2': 2.9,
     'gla_ba': 7.247,
     'gla_norm_g': 21.625}
    for name, (base, spread) in spreads.items():
        noise = np.random.default_rng([zlib.crc32(name.encode()), seed]).standard_normal(out[name].shape)
        drawn = base * np.exp(spread * noise) if base else spread * noise
        out[name] = jnp.asarray(drawn.astype(out[name].dtype))
    for name, factor in factors.items():
        out[name] = (out[name] * factor).astype(out[name].dtype)
    return out
```

```python
import math
from contextlib import ExitStack

import numpy as np
import concourse.bass as bass
from concourse import mybir

F32 = mybir.dt.float32
I32 = mybir.dt.int32
F32R = mybir.dt.float32r
ALU = mybir.AluOpType
ACT = mybir.ActivationFunctionType
AX = mybir.AxisListType.X

P = 128
D = 1024
S = 256
T = S // P
KC = D // P
N = 512
DEPTH = 2
ALPHA = (2 * DEPTH) ** 0.25
EPS = 1e-5
NEG = -1e30
THETA = 500000.0

AH, AQ, AV = 4, 32, 64
BH, BD = 6, 64
CH, CK, CV, CR = 4, 48, 96, 16
TAU = 16.0
XH, XD = 4, 256
A_Q, A_K, A_VAL = 0, 256, 512
B_Q, B_K, B_VAL = 768, 1152, 1536
C_Q, C_K, C_VAL, C_G, C_RANK = 1920, 2112, 2304, 2688, 3072
IN_COLS = 3088
F_DENSE = 2816
NE, F_MOE = 8, 3584
EXTRA = 3
ROPE = 8

DENSE_SLOTS = 3
RAW_SLOTS = 7
SPLIT_SLOTS = 3
HALF = KC * N // 2
IN_P, KV_P, OUT_P, Q_P, O_P = 6, 4, 2, 2, 2
MIX_PANELS = IN_P + KV_P + OUT_P + Q_P + O_P
FFN_CHUNKS = -(-F_DENSE // N)
W2_P = -(-(F_DENSE // P) // 4)
L1 = MIX_PANELS + 2 * FFN_CHUNKS + W2_P
L1_ACC = MIX_PANELS - KV_P + 2 * FFN_CHUNKS
DENSE_PANELS = L1 + MIX_PANELS
MOE_PAIRS = F_MOE // N
ITEM_HALVES = 6 * MOE_PAIRS
UNITS = 7
TURNED_AT = [4 * n + 11 for n in range(MOE_PAIRS - 1)] + [35]
GATHERED_AT = [37, 38]
ADDED_AT = [6, 7, 8, 9]
LEVELS = 7
GSTEPS = LEVELS + 2
MAGIC = 1.5 * 2.0 ** 23
PI2 = (6.28125, 0.0019350051879882812, 3.0198e-07)


def shape_constants():
    i = np.arange(P)
    q = np.arange(S).reshape(T, P).T
    k = np.arange(S)
    dist = q[:, :, None] - k[None, None, :]
    mask_a = np.where(dist >= 0, 0.0, NEG).astype(np.float32)
    times = ((dist >= 0) & (dist <= 128)).astype(np.int64)
    for dilation in (4, 16):
        times = times + ((dist >= 0) & (dist % dilation == 0))
    mask_b = np.where(times > 0, np.log(np.maximum(times, 1)), NEG).astype(np.float32)
    level = np.zeros((P, LEVELS, P), np.int32)
    for v in range(LEVELS):
        half = (P // 2) >> v
        block = i // (2 * half)
        upper = (i // half) % 2
        level[:, v, :] = (block[:, None] == block[None, :]) & (upper[:, None] == 0) & (upper[None, :] == 1)
    square = np.stack([np.eye(P), i[:, None] < i[None, :], np.ones((P, P)),
                       np.broadcast_to(i[None, :], (P, P))], 1).astype(np.float32)
    freq = (THETA ** (-np.arange(0, 2 * ROPE, 2, dtype=np.float32) / np.float32(2 * ROPE))).astype(np.float32)
    e = np.arange(NE, dtype=np.float32)
    rows = np.concatenate([freq, NE - e, e, np.arange(EXTRA, dtype=np.float32)])
    rows = np.broadcast_to(rows[None, :], (P, rows.size)).astype(np.float32)
    return {"mask_a": mask_a, "mask_b": mask_b, "level": level, "square": square,
            "rows": np.ascontiguousarray(rows)}


def bass_decoder(nc, a, out):
    ctx = ExitStack()
    with ctx:
        def sb(name, shape, dt=F32):
            return ctx.enter_context(nc.sbuf_tensor(name, shape, dt))

        def sem(name):
            return ctx.enter_context(nc.semaphore(name))

        ring = sb("ring", [P, RAW_SLOTS, HALF])
        ringf = ring[:, :, :].rearrange("p s n -> p (s n)")
        x = sb("x", [P, T, D])
        ln_gb = sb("ln_gb", [P, 2, D])
        square = sb("square", [P, 4, P])
        ident, before, ones, iota = (square[:, n, :] for n in range(4))
        rows = sb("rows", [P, ROPE + 2 * NE + EXTRA])
        freq = rows[:, 0:ROPE]
        desc = rows[:, ROPE:ROPE + NE]
        eid = rows[:, ROPE + NE:ROPE + 2 * NE]
        w_router = sb("w_router", [P, KC, NE])
        stats = sb("stats", [P, T, 2, 6])
        mv = sb("mv", [P, T, 2])
        var = sb("var", [P, 8])
        rstd = sb("rstd", [P, 8])
        mhalf = sb("mhalf", [P, 8])
        lg = sb("lg", [P, 2, T, NE])
        oh = sb("oh", [P, 2, T, NE])
        rtmp = sb("rtmp", [P, T, NE])
        rmx = sb("rmx", [P, 4, T])
        chosen = sb("chosen", [P, T, NE])
        gates = sb("gates", [P, T, 12])
        slot = sb("slot", [P, T, 12])
        cnt = sb("cnt", [P, 4, NE])
        wr = sb("wr", [P, EXTRA, NE])
        table = sb("table", [P, 5])
        table_i = sb("table_i", [P, 5], I32)

        with ExitStack() as scope:
            def sbe(name, shape, dt=F32):
                return scope.enter_context(nc.sbuf_tensor(name, shape, dt))

            w_hi = sbe("w_hi", [P, SPLIT_SLOTS, HALF], F32R)
            w_lo = sbe("w_lo", [P, SPLIT_SLOTS, HALF], F32R)
            he_hi = sbe("he_hi", [P, F_MOE // P, P], F32R)
            he_lo = sbe("he_lo", [P, F_MOE // P, P], F32R)
            xe_hi = sbe("xe_hi", [P, KC, P], F32R)
            xe_lo = sbe("xe_lo", [P, KC, P], F32R)
            accum = sbe("accum", [P, T, D])
            acc = accum[:, :, :]
            y = sbe("y", [P, D])
            sge = sbe("sge", [P, 2, N])
            hge = sbe("hge", [P, 2, N])
            sel = sbe("sel", [P, T, P])
            gsel = sbe("gsel", [P, T, P])
            gselT = sbe("gselT", [P, T * P])

        late = sb("late", [P, 4 * KC * N])[:, :]
        tr = late[:, 0:4096].rearrange("p (b s) -> p b s", b=16)
        kT = late[:, 4096:6144].rearrange("p (c s) -> p c s", c=KC)
        v_mem = late[:, 6144:8192].rearrange("p (t d) -> p t d", t=T)
        o_tok = late[:, 8192:10240].rearrange("p (t d) -> p t d", t=T)
        dec = late[:, 10240:14336].rearrange("p (v n) -> p v n", v=8)
        s4 = late[:, 14336:16384].rearrange("p (b i k) -> p b i k", b=2, i=4)
        hg = dec[:, 0:4, :].rearrange("p (b t) n -> p b t n", b=2)
        sg = s4[:, 0, :, :].rearrange("p i k -> p (i k)").rearrange("p (t n) -> p t n", t=T)
        xT = sb("xT", [P, KC, S])
        k_mem = xT[:, :, :].rearrange("p c s -> p (c s)").rearrange("p (t d) -> p t d", t=T)
        memT = sb("memT", [P, KC, S])
        h = sb("h", [P, T, IN_COLS])
        hflat = h[:, :, :].rearrange("p t n -> p (t n)")
        hT = hflat[:, 0:F_DENSE // P * S].rearrange("p (c s) -> p c s", s=S)
        q_tok = h[:, :, 0:D]
        o_xa = h[:, :, D:2 * D]
        cpad = sb("cpad", [P, T, 3 * CH, 64])
        qk = sb("qk", [P, 2, 2, 2 * S])
        spare = ringf[:, DENSE_SLOTS * KC * N:]
        st = spare[:, 0:8 * P].rearrange("p (h b s) -> p h b s", h=2, b=4)
        stx = spare[:, 8 * P:12 * P].rearrange("p (h b s) -> p h b s", h=2, b=2)
        pT = qk[:, 0, :, :].rearrange("p n s -> p (n s)").rearrange("p (c s) -> p c s", c=8)
        mask_a = sb("mask_a", [P, T, S])
        mask_b = sb("mask_b", [P, T, S])
        level = sb("level", [P, LEVELS, P], I32)
        lamv = sb("lamv", [P, DEPTH, 4, AQ])
        g_a = sb("g_a", [P, DEPTH, AV])
        g_c = sb("g_c", [P, DEPTH, CV])
        ba = sb("ba", [P, DEPTH, CH * CK])
        wa2 = sb("wa2", [CR, DEPTH, CH * CK])
        w_rank = spare[:, 12 * P:14 * P].rearrange("p (l c r) -> p l c r", l=DEPTH, c=KC)
        pos_i = sb("pos_i", [P, T], I32)
        pos = sb("pos", [P, T])
        ang = sb("ang", [P, 2, T, ROPE])
        angr = sb("angr", [P, 2, T, ROPE])
        trig = sb("trig", [P, 2, T, ROPE])
        rt = s4[:, 0, :, 0:T * 24 * 4].rearrange("p n (t k) -> p n t k", t=T)
        rank = sb("rank", [P, T, CR])
        rankT = spare[0:CR, 14 * P:16 * P]
        zz = dec[:, 0:3, 0:T * CH * CK]
        oa_sq = spare[:, 0:T * S].rearrange("p (t n) -> p t n", t=T)
        lamp = sb("lamp", [P, 2, AQ])
        lams = sb("lams", [P, 4])
        nmax = sb("nmax", [P, 2, 4])
        sums = sb("sums", [P, 4 * UNITS])
        rsum = sb("rsum", [P, 4 * UNITS])

        ps = ctx.enter_context(nc.psum_tensor("ps", [P, 8, N], F32))

        x_in, mem_in = sem("x_in"), sem("mem_in")
        pos_in, const_in = sem("pos_in"), sem("const_in")
        ln_in = sem("ln_in")
        panel_in = [sem(f"panel_in{s}") for s in range(DENSE_SLOTS)]
        panel_used = sem("panel_used")
        acc_ready = [sem(f"acc_ready{b}") for b in range(4)]
        acc_taken = [sem(f"acc_taken{b}") for b in range(4)]
        tp_ready = [sem(f"tp_ready{b}") for b in range(4)]
        tp_taken = [sem(f"tp_taken{b}") for b in range(4)]
        h_act, h_dve = sem("h_act"), sem("h_dve")
        kv_psum = sem("kv_psum")
        kv_act, kv_dve = sem("kv_act"), sem("kv_dve")
        q_act, q_dve = sem("q_act"), sem("q_dve")
        rank_psum, rank_sb = sem("rank_psum"), sem("rank_sb")
        rankT_psum, rankT_sb = sem("rankT_psum"), sem("rankT_sb")
        z_psum, z_abs, z_ln = sem("z_psum"), sem("z_abs"), sem("z_ln")
        angles, trig_ready = sem("angles"), sem("trig_ready")
        lam_dots, lam_exps = sem("lam_dots"), sem("lam_exps")
        rope_done = sem("rope_done")
        cqk_ready, decay_ready = sem("cqk_ready"), sem("decay_ready")
        tr_psum = [sem(f"tr_psum{b}") for b in range(4)]
        tr_sb = [sem(f"tr_sb{b}") for b in range(4)]
        decT_psum, decT_sb = sem("decT_psum"), sem("decT_sb")
        gate_silu = sem("gate_silu")
        scores_ready, score_taken = sem("scores_ready"), sem("score_taken")
        max_ready, probs_ready, diff_ready = sem("max_ready"), sem("probs_ready"), sem("diff_ready")
        turn_ready, turn_taken, pv_done = sem("turn_ready"), sem("turn_taken"), sem("pv_done")
        oa_taken = sem("oa_taken")
        dec_diff, dec_exp = sem("dec_diff"), sem("dec_exp")
        level_ready, level_scores, level_taken = sem("level_ready"), sem("level_scores"), sem("level_taken")
        gla_out, gla_square = sem("gla_out"), sem("gla_square")
        mixed = sem("mixed")
        xs_ready, xmax_ready, xp_ready = sem("xs_ready"), sem("xmax_ready"), sem("xp_ready")
        xturn_ready, xturn_taken = sem("xturn_ready"), sem("xturn_taken")
        xo_ready, xo_taken = sem("xo_ready"), sem("xo_taken")
        var_ready, rstd_ready = sem("var_ready"), sem("rstd_ready")
        ln_done = sem("ln_done")
        silu_ready, hg_ready = sem("silu_ready"), sem("hg_ready")
        hT_psum = [sem(f"hT_psum{t}") for t in range(T)]
        hT_sb = [sem(f"hT_sb{t}") for t in range(T)]
        w2_ready = sem("w2_ready")
        logit_psum, chosen_ready, rank2_psum = sem("logit_psum"), sem("chosen_ready"), sem("rank2_psum")
        gate_diff, gate_exp = sem("gate_diff"), sem("gate_exp")
        table_ready = sem("table_ready")
        raw_in = [sem(f"raw_in{s}") for s in range(RAW_SLOTS)]
        hi_ready, lo_ready = sem("hi_ready"), sem("lo_ready")
        half_used = sem("half_used")
        he_split, xe_split = sem("he_split"), sem("xe_split")
        sel_ready, gsel_ready = sem("sel_ready"), sem("gsel_ready")
        g_ready, g_taken = sem("g_ready"), sem("g_taken")
        u_ready, he_ready = sem("u_ready"), sem("he_ready")
        misc_ready = [sem(f"misc_ready{b}") for b in range(2)]
        misc_taken = [sem(f"misc_taken{b}") for b in range(2)]
        y_ready, y_act, y_dve = sem("y_ready"), sem("y_act"), sem("y_dve")
        acc_init = sem("acc_init")
        out_done = sem("out_done")
        vstep = sem("vstep")
        sstep = sem("sstep")
        pstep = sem("pstep")

        CONSTS = 14
        POWERS = 2 + 3 * T
        TURN = {"x0": 0, "mem": 1}
        for l in range(DEPTH):
            for n, name in enumerate(("k", "mix", "x1", "q", "xa", "x2", "x3")):
                TURN[name, l] = 2 + 7 * l + n

        def panel(l, n):
            return l * L1 + n

        def acc_use(l, n):
            return l * L1_ACC + (n if n < IN_P else n - KV_P)

        def w_panel(l, n):
            def cols(w, c0, width=N):
                return w.rearrange("(c p) n -> p c n", p=P)[:, :, c0:c0 + width]
            for w, count in ((a["w_in"][l], IN_P), (a["xa_wkv"][l], KV_P), (a["w_out"][l], OUT_P),
                             (a["xa_wq"][l], Q_P), (a["xa_wo"][l], O_P)):
                if n < count:
                    return cols(w, n * N)
                n -= count
            if n < 2 * FFN_CHUNKS:
                width = min(N, F_DENSE - n // 2 * N)
                return cols(a["ffd_w13"][0], (n % 2) * F_DENSE + n // 2 * N, width)
            n -= 2 * FFN_CHUNKS
            r0, r1 = 4 * n, min(4 * n + 4, F_DENSE // P)
            return a["ffd_w2"][0].rearrange("(c p) n -> p c n", p=P)[:, r0:r1, :]

        def slot_view(p, src_shape):
            _, c, n = src_shape
            at = p % DENSE_SLOTS * KC * N
            return ringf[:, at:at + c * n].rearrange("p (c n) -> p c n", c=c)

        def half_view(buffer, q, slots):
            return buffer[:, q % slots, :].rearrange("p (c n) -> p c n", c=4 if q < 4 * MOE_PAIRS else 2)

        def piece_bank(i):
            return 1 if i <= 4 else 5 if i % 2 else 7

        def score_view(u, i):
            if u < 4:
                return ps[:, 4 + i, 0:P * (u % 2 + 1)]
            j, t = divmod(i, 2)
            return ps[:, 4 + 2 * j, P * t:P * (2 * t + 1)]

        def cross_bank(t, i):
            return ps[:, 4 + 2 * t + i // 2, i % 2 * S:(i % 2 + 1) * S]

        block = ctx.enter_context(nc.Block())

        @block.sync
        def _(sp):
            sp.dma_start(x[:, :, :], a["x"][0].rearrange("(t p) d -> p t d", p=P)).then_inc(x_in, 16)
            sp.dma_start(square[:, :, :], a["square"]).then_inc(x_in, 16)

            def load_ln(k):
                l, s = divmod(k, 3)
                g, b = (("ln_mix_g", "ln_mix_b"), ("ln_xa_g", "ln_xa_b"), ("ln_ffn_g", "ln_ffn_b"))[s]
                if k:
                    sp.wait_ge(ln_done, T * k)
                for n, w in enumerate((g, b)):
                    sp.dma_start(ln_gb[:, n, :], a[w][l:l + 1, :].to_broadcast([P, D])).then_inc(ln_in, 16)

            def dense(l, n):
                p = panel(l, n)
                src = w_panel(l, n)
                if p >= DENSE_SLOTS:
                    sp.wait_ge(panel_used, p - DENSE_SLOTS + 1)
                sp.dma_start(slot_view(p, src.shape), src).then_inc(panel_in[p % DENSE_SLOTS], 16)

            for l in range(DEPTH):
                for n in range(L1 if l == 0 else MIX_PANELS):
                    dense(l, n)
                    if l == 0 and n == 1:
                        sp.dma_start(o_tok, a["mem"][0].rearrange("(t p) d -> p t d", p=P)).then_inc(mem_in, 16)
                    if n == IN_P + KV_P + OUT_P - 1:
                        load_ln(3 * l)
                    if n == MIX_PANELS - 1:
                        load_ln(3 * l + 1)
                    if n == L1 - 1:
                        load_ln(3 * l + 2)

            def item_half(q, i, e):
                if q < 4 * MOE_PAIRS:
                    c0 = (q // 2 % 2) * F_MOE + q // 4 * N
                    r = 4 * (q % 2)
                    src = a["moe_w13"][0, e].rearrange("(c p) n -> p c n", p=P)[:, r:r + 4, c0:c0 + N]
                else:
                    r = 2 * (q - 4 * MOE_PAIRS)
                    src = a["moe_w2"][0, e].rearrange("(c p) n -> p c n", p=P)[:, r:r + 2, :]
                sp.dma_start(half_view(ring, q, RAW_SLOTS), src).then_inc(raw_in[q % RAW_SLOTS], 16)

            def item_halves(i, e, first=0):
                for q in range(first, ITEM_HALVES):
                    sp.wait_ge(lo_ready, ITEM_HALVES * i + (q - RAW_SLOTS + 1))
                    item_half(q, i, e)

            for q in range(RAW_SLOTS - 1):
                last = max(p for p in range(DENSE_PANELS) if p % DENSE_SLOTS == q // 2)
                sp.wait_ge(panel_used, last + 1)
                item_half(q, 0, 0)
            load_ln(5)
            item_half(RAW_SLOTS - 1, 0, 0)
            item_halves(0, 0, RAW_SLOTS)
            with sp.Fori(1, NE) as i:
                item_halves(i, i)
            sp.wait_ge(table_ready, 1)
            n_items = sp.value_load(table_i[0:1, 0:1], min_val=NE, max_val=NE + EXTRA)
            with sp.If(n_items > NE):
                with sp.Fori(NE, n_items) as i:
                    e = sp.value_load(table_i[0:1, bass.ds(i - (NE - 1), 1)], min_val=0, max_val=NE - 1)
                    item_halves(i, e)
            sp.wait_ge(ln_done, T * 6)
            sp.dma_start(out[0].rearrange("(t p) d -> p t d", p=P), acc).then_inc(out_done, 16)
            sp.wait_ge(out_done, 16)

        @block.gpsimd
        def _(pool):
            pool.memset(mhalf[:, :], -0.5).then_inc(pstep, 1)
            pool.memset(cpad[:, :, :, CK:64], 0.0).then_inc(pstep, 1)
            pool.wait_ge(pstep, 2)
            for k in range(POWERS * DEPTH):
                c = slice(0, 8) if k % POWERS < 2 else slice(k % 2, k % 2 + 1)
                pool.wait_ge(var_ready, k + 1)
                pool.tensor_tensor(rstd[:, c], var[:, c], mhalf[:, c], ALU.pow).then_inc(rstd_ready, 1)

        @block.scalar
        def _(act):
            step = [0]

            def done(ins):
                step[0] += 1
                ins.then_inc(sstep, 1)
                act.wait_ge(sstep, step[0])

            def take(l, n, t, dst, signal):
                u = acc_use(l, n)
                b = 2 * (u % 2) + t
                act.wait_ge(acc_ready[b], u // 2 + 1)
                act.copy(dst, ps[:, b, :]).then_inc(signal, 1)
                act.wait_ge(signal, signal_count[signal.name] + 1)
                signal_count[signal.name] += 1
                act.sem_inc(acc_taken[b], 1)

            signal_count = {h_act.name: 0, q_act.name: 0}

            def turn(m, dst, tiles=range(T)):
                for t in tiles:
                    b = 2 * t
                    act.wait_ge(tp_ready[b], m + 1)
                    act.copy(dst[:, 0:4, t * P:(t + 1) * P],
                             ps[:, 4 + b, :].rearrange("p (c s) -> p c s", c=4)).then_inc(tp_taken[b], 1)

            def take_piece(l, i):
                act.wait_ge(kv_psum, 2 * KV_P * l + i + 1)
                n = i // 2
                dst = k_mem[:, 0, n * N:(n + 1) * N] if n < 2 else v_mem[:, 0, (n - 2) * N:(n - 1) * N]
                act.copy(dst, ps[:, piece_bank(i), :]).then_inc(kv_act, 1)

            for n, (dst, src) in enumerate((
                (pos_i[:, :], a["positions"][0].rearrange("(t p) -> p t", p=P)),
                (rows[:, :], a["rows"]),
            )):
                act.dma_start(dst, src, allow_slow_non_contiguous=(n == 0)).then_inc(pos_in, 16)
            turn(TURN["x0"], xT)
            act.wait_ge(panel_in[0], 16)
            for dst, src in (
                (mask_a[:, :, :], a["mask_a"]), (mask_b[:, :, :], a["mask_b"]), (level[:, :, :], a["level"]),
                (lamv[:, :, 0, :], a["lam_q1"].unsqueeze(0).to_broadcast([P, DEPTH, AQ])),
                (lamv[:, :, 1, :], a["lam_k1"].unsqueeze(0).to_broadcast([P, DEPTH, AQ])),
                (lamv[:, :, 2, :], a["lam_q2"].unsqueeze(0).to_broadcast([P, DEPTH, AQ])),
                (lamv[:, :, 3, :], a["lam_k2"].unsqueeze(0).to_broadcast([P, DEPTH, AQ])),
                (g_a[:, :, :], a["diff_norm_g"].unsqueeze(0).to_broadcast([P, DEPTH, AV])),
                (g_c[:, :, :], a["gla_norm_g"].unsqueeze(0).to_broadcast([P, DEPTH, CV])),
                (ba[:, :, :], a["gla_ba"].unsqueeze(0).to_broadcast([P, DEPTH, CH * CK])),
                (wa2[:, :, :], a["gla_wa2"].rearrange("l r n -> r l n")),
                (w_router[:, :, :], a["moe_router"][0].rearrange("(c p) e -> p c e", p=P)),
            ):
                act.dma_start(dst, src).then_inc(const_in, 16)
            for l in range(DEPTH):
                act.dma_start(w_rank[:, l, :, :], a["w_in"][l].rearrange("(c p) n -> p c n", p=P)[:, :, C_RANK:])\
                    .then_inc(const_in, 16)
            act.wait_ge(angles, 1)
            act.activation(trig[:, :, :, :], angr[:, :, :, :], ACT.Sin).then_inc(trig_ready, 1)

            for l in range(DEPTH):
                for n in range(IN_P):
                    take(l, n, 0, h[:, 0, n * N:(n + 1) * N], h_act)
                    if l == 0 and n == 1:
                        turn(TURN["mem"], memT)
                    if l == 1 and n == 1:
                        turn(TURN["x3", l - 1], xT, (1,))
                    if n == 2:
                        act.wait_ge(lam_dots, l + 1)
                        act.activation(lams[:, 0:2], lams[:, 0:2], ACT.Exp).then_inc(lam_exps, 1)
                    if n == 4:
                        act.wait_ge(h_dve, IN_P * l + 5)
                        if l == 0:
                            act.wait_ge(pstep, 2)
                        else:
                            act.wait_ge(tr_psum[2], 2 * l)
                        act.mul(cpad[:, :, 0:CH, 0:CK], h[:, :, C_Q:C_K].rearrange("p t (h k) -> p t h k", h=CH),
                                CK ** -0.5).then_inc(cqk_ready, 1)
                        act.copy(cpad[:, :, CH:2 * CH, 0:CK],
                                 h[:, :, C_K:C_VAL].rearrange("p t (h k) -> p t h k", h=CH)).then_inc(cqk_ready, 1)
                act.wait_ge(rank_psum, l + 1)
                act.copy(rank[:, :, :], ps[:, 0, 0:T * CR].rearrange("p (t r) -> p t r", t=T)).then_inc(rank_sb, 1)
                for r in (0, 2):
                    act.wait_ge(tr_psum[r], 2 * l + 1)
                    act.copy(tr[:, 2 * r:2 * r + 2, :], ps[:, 4 + r, :].rearrange("p (b s) -> p b s", b=2))\
                        .then_inc(tr_sb[r], 1)
                act.wait_ge(rankT_psum, l + 1)
                act.copy(rankT, ps[0:CR, 0, P:P + S]).then_inc(rankT_sb, 1)
                for r in (4, 6):
                    act.wait_ge(tr_psum[r % 4], 2 * l + 2)
                    act.copy(tr[:, 2 * r:2 * r + 2, :], ps[:, 4 + r % 4, :].rearrange("p (b s) -> p b s", b=2))\
                        .then_inc(tr_sb[r % 4], 1)

                def exps(u):
                    act.wait_ge(max_ready, UNITS * l + u + 1)
                    for i in range(4):
                        w = P * ((u if u < 4 else i) % 2 + 1)
                        ins = act.activation(s4[:, u % 2, i, 0:w], s4[:, u % 2, i, 0:w], ACT.Exp,
                                             bias=nmax[:, u % 2, i:i + 1], accum_out=sums[:, 4 * u + i:4 * u + i + 1])
                    ins.then_inc(probs_ready, 1)

                exps(0)
                act.wait_ge(z_abs, l + 1)
                done(act.activation(zz[:, 1, :], zz[:, 1, :], ACT.Exp, scale=-1.0))
                act.activation(zz[:, 1, :], zz[:, 1, :], ACT.Ln, bias=1.0).then_inc(z_ln, 1)
                take_piece(l, 0)
                for u in range(UNITS):
                    if u + 1 < UNITS:
                        exps(u + 1)
                    act.wait_ge(turn_ready, UNITS * l + u + 1)
                    c0, c1 = (0, 2) if u < 4 and u % 2 == 0 else (2, 6) if u < 4 else (0, 6)
                    if c0 == 0:
                        ins = act.copy(pT[:, 0:2, :], ps[:, 2, 0:2 * P].rearrange("p (c s) -> p c s", c=2))
                        if c1 > 2:
                            done(ins)
                    if c1 == 6:
                        ins = act.copy(pT[:, 2:6, :], ps[:, 3, :].rearrange("p (c s) -> p c s", c=4))
                    ins.then_inc(turn_taken, 1)
                    if u % 2:
                        take_piece(l, u + 1)
                    if u == 0:
                        act.wait_ge(decT_psum, l + 1)
                        act.copy(tr[:, 14:16, :], ps[:, 3, :].rearrange("p (b s) -> p b s", b=2)).then_inc(decT_sb, 1)
                    if u == 4:
                        act.wait_ge(dec_diff, l + 1)
                        done(act.activation(dec, dec, ACT.Abs))
                    if u == 5:
                        act.activation(dec, dec, ACT.Exp, scale=-1.0).then_inc(dec_exp, 1)
                act.activation(h[:, :, C_G:C_RANK], h[:, :, C_G:C_RANK], ACT.Silu).then_inc(gate_silu, 1)
                act.wait_ge(gla_out, l + 1)
                act.activation(zz[:, 0:2, :], ps[:, 2:4, 0:CH * CV], ACT.Square).then_inc(gla_square, 1)
                turn(TURN["k", l], kT)
                turn(TURN["mix", l], xT)
                turn(TURN["x1", l], xT, (0,))

                def cross_exps(t):
                    act.wait_ge(xmax_ready, T * l + t + 1)
                    for i in range(XH):
                        ins = act.activation(s4[:, t, i, :], cross_bank(t, i), ACT.Exp, bias=nmax[:, t, i:i + 1],
                                             scale=XD ** -0.5, accum_out=sums[:, 4 * t + i:4 * t + i + 1])
                    ins.then_inc(xp_ready, 1)

                def cross_turned(t):
                    act.wait_ge(xturn_ready, T * l + t + 1)
                    act.copy(pT, ps[:, 4 + 2 * t:6 + 2 * t, :].rearrange("p b (c s) -> p (b c) s", c=4))\
                        .then_inc(xturn_taken, 1)

                for n in range(Q_P):
                    take(l, IN_P + KV_P + OUT_P + n, 0, q_tok[:, 0, n * N:(n + 1) * N], q_act)
                turn(TURN["x1", l], xT, (1,))
                turn(TURN["q", l], xT, (0,))
                cross_exps(0)
                cross_turned(0)
                turn(TURN["q", l], xT, (1,))
                cross_exps(1)
                turn(TURN["xa", l], xT, (0,))
                cross_turned(1)
                turn(TURN["xa", l], xT, (1,))
                turn(TURN["x2", l], xT, (0,))
                if l == 1:
                    turn(TURN["x2", l], xT, (1,))
                if l == 0:
                    for n in range(FFN_CHUNKS + 1):
                        if n < FFN_CHUNKS:
                            w = min(N, F_DENSE - n * N)
                            for t in range(T):
                                u = acc_use(l, MIX_PANELS + 2 * n)
                                act.wait_ge(acc_ready[t], u // 2 + 1)
                                if n >= 1:
                                    act.wait_ge(hg_ready, 2 * (n - 1) + t + 1)
                                act.activation(sg[:, t, 0:w], ps[:, t, 0:w], ACT.Silu).then_inc(silu_ready, 1)
                                act.wait_ge(silu_ready, 2 * n + t + 1)
                                act.sem_inc(acc_taken[t], 1)
                                if n == 0 and t == 0:
                                    turn(TURN["x2", l], xT, (1,))
                        if n >= 1:
                            m = n - 1
                            c = min(4, F_DENSE // P - 4 * m)
                            act.wait_ge(hT_psum[0], m + 1)
                            act.copy(hT[:, 4 * m:4 * m + c, 0:P],
                                     ps[:, 4 + 2 * (m % 2), 0:c * P].rearrange("p (c s) -> p c s", c=c))\
                                .then_inc(hT_sb[0], 1)
                    turn(TURN["x3", l], xT, (0,))

            act.wait_ge(gate_diff, 1)
            act.activation(rmx[:, 2, :], rmx[:, 2, :], ACT.Exp).then_inc(gate_exp, 1)

            def misc(j, i, dst, groups, signal):
                q = 2 + j
                b, uses = q % 2, q // 2
                act.wait_ge(misc_ready[b], (uses + 1) if j < 0 else 7 * i + (uses + 1))
                act.copy(dst, ps[:, 6 + b, 0:groups * P].rearrange("p (c s) -> p c s", c=groups)).then_inc(signal, 1)

            def gather_high(i, j, g):
                misc(j + g, i, xe_hi[:, 4 * g:4 * g + 4, :], 4, xe_split)

            for g in range(2):
                gather_high(0, -2, g)
            act.sem_inc(g_taken, 1)
            act.sem_inc(y_act, 1)
            act.wait_ge(table_ready, 1)

            def high(q, i, first=False):
                act.wait_ge(raw_in[q % RAW_SLOTS], 96 * i + 16 * (q // RAW_SLOTS + 1))
                act.wait_ge(half_used, ITEM_HALVES * i + (q + 1))
                act.copy(w_hi[:, q % SPLIT_SLOTS, :], ring[:, q % RAW_SLOTS, :]).then_inc(hi_ready, 1)

            def take_y(i):
                act.wait_ge(y_ready, i + 1)
                act.copy(y[:, 0:N], ps[:, 4, :]).then_inc(y_act, 1)

            def item(i, first=False):
                for q in range(ITEM_HALVES):
                    high(q, i)
                    if q == SPLIT_SLOTS - 1 and not first:
                        take_y(i - 1)
                    if q % 4 == 0 and 4 <= q <= 4 * MOE_PAIRS:
                        n = q // 4 - 1
                        act.wait_ge(g_ready, MOE_PAIRS * i + (n + 1))
                        if n >= 2:
                            act.wait_ge(he_ready, MOE_PAIRS * i + n)
                        act.activation(sge[:, n % 2, :], ps[:, 2 * (n % 2), :], ACT.Silu).then_inc(g_taken, 1)
                    if q in TURNED_AT:
                        n = TURNED_AT.index(q)
                        misc(n, i, he_hi[:, 4 * n:4 * n + 4, :], 4, he_split)
                    if q in GATHERED_AT:
                        gather_high(i, 7, GATHERED_AT.index(q))
                misc(9, i, gselT[:, :].rearrange("p (c s) -> p c s", c=2), 2, misc_taken[1])

            item(0, first=True)
            n_items = act.value_load(table_i[0:1, 0:1], min_val=NE, max_val=NE + EXTRA)
            last = act.value_load(table_i[0:1, 4:5], min_val=NE - 1, max_val=NE + EXTRA - 1)
            with act.Fori(1, n_items) as i:
                item(i)
            take_y(last)

        @block.vector
        def _(dve):
            step = [0]

            def done(ins):
                step[0] += 1
                ins.then_inc(vstep, 1)
                dve.wait_ge(vstep, step[0])

            signal_count = {h_dve.name: 0, q_dve.name: 0}

            def take(l, n, t, dst, signal):
                u = acc_use(l, n)
                b = 2 * (u % 2) + t
                dve.wait_ge(acc_ready[b], u // 2 + 1)
                dve.tensor_copy(dst, ps[:, b, :]).then_inc(signal, 1)
                signal_count[signal.name] += 1
                dve.wait_ge(signal, signal_count[signal.name])
                dve.sem_inc(acc_taken[b], 1)

            def turn(m, dst, tiles=range(T)):
                for t in tiles:
                    b = 2 * t + 1
                    dve.wait_ge(tp_ready[b], m + 1)
                    dve.tensor_copy(dst[:, 4:8, t * P:(t + 1) * P],
                                    ps[:, 4 + b, :].rearrange("p (c s) -> p c s", c=4)).then_inc(tp_taken[b], 1)

            def norm_of(k, n, width, meanwhile=None):
                done(dve.tensor_scalar(var[:, 0:n], var[:, 0:n], 1.0 / width, EPS, ALU.mult, ALU.add))
                dve.sem_inc(var_ready, 1)
                if meanwhile:
                    meanwhile()
                dve.wait_ge(rstd_ready, k + 1)

            def layer_norm(k, xx, t):
                xx = xx[:, t, :]
                for g in range(2):
                    ins = dve.bn_stats(stats[:, t, g, :], xx[:, g * N:(g + 1) * N])
                done(ins)
                done(dve.bn_aggr(mv[:, t, :], stats[:, t, :, :]))
                done(dve.tensor_scalar(var[:, t:t + 1], mv[:, t, 1:2], EPS, None, ALU.add))
                dve.sem_inc(var_ready, 1)
                l, s = divmod(k, 3)
                dve.wait_ge(rstd_ready, POWERS * l + 3 + T * s + t)
                done(dve.tensor_scalar(xx, xx, mv[:, t, 0:1], rstd[:, t:t + 1], ALU.subtract, ALU.mult))
                dve.wait_ge(ln_in, 32 * (k + 1))
                for op, n in ((ALU.mult, 0), (ALU.add, 1)):
                    done(dve.tensor_tensor(xx, xx, ln_gb[:, n, :], op))
                dve.sem_inc(ln_done, 1)

            def residual(l, n0, n, t):
                u = acc_use(l, n0 + n)
                b = 2 * (u % 2) + t
                dve.wait_ge(acc_ready[b], u // 2 + 1)
                xs = x[:, t, n * N:(n + 1) * N]
                done(dve.scalar_tensor_tensor(xs, xs, ALPHA, ps[:, b, :], ALU.mult, ALU.add))
                dve.sem_inc(acc_taken[b], 1)

            def take_piece(l, i):
                dve.wait_ge(kv_psum, 2 * KV_P * l + i + 1)
                n = i // 2
                dst = k_mem[:, 1, n * N:(n + 1) * N] if n < 2 else v_mem[:, 1, (n - 2) * N:(n - 1) * N]
                dve.tensor_copy(dst, ps[:, piece_bank(i), :]).then_inc(kv_dve, 1)

            turn(TURN["x0"], xT)
            dve.wait_ge(pos_in, 32)
            done(dve.tensor_copy(pos[:, :], pos_i[:, :]))
            done(dve.tensor_tensor(ang[:, 0, :, :], pos[:, :].unsqueeze(2).to_broadcast([P, T, ROPE]),
                                   freq.unsqueeze(1).to_broadcast([P, T, ROPE]), ALU.mult))
            done(dve.tensor_scalar(ang[:, 1, :, :], ang[:, 0, :, :], 1.0 / (2 * math.pi), MAGIC, ALU.mult, ALU.add))
            done(dve.tensor_scalar(ang[:, 1, :, :], ang[:, 1, :, :], MAGIC, None, ALU.subtract))
            af = ang[:, :, :, :].rearrange("p a t f -> p a (t f)")
            for c in PI2:
                done(dve.scalar_tensor_tensor(af[:, 0, :], af[:, 1, :], -c, af[:, 0, :], ALU.mult, ALU.add))
            done(dve.tensor_scalar(angr[:, 0, :, :], ang[:, 0, :, :], math.pi, -math.pi, ALU.min, ALU.max))
            rf = angr[:, :, :, :].rearrange("p a t f -> p a (t f)")
            done(dve.scalar_tensor_tensor(rf[:, 1, :], rf[:, 0, :], -1.0, rf[:, 0, :], ALU.mult, ALU.min))
            done(dve.tensor_scalar(angr[:, 1, :, :], angr[:, 1, :, :], math.pi / 2, None, ALU.add))
            dve.sem_inc(angles, 1)

            def rope(base, heads, width, pairs, stride):
                v = h[:, :, base:base + heads * width].rearrange("p t (h k) -> p t h k", k=width)
                x1, x2 = v[:, :, :, 0:pairs], v[:, :, :, pairs:2 * pairs]
                shape = [P, T, heads, pairs]
                sn, cs = (trig[:, n, :, ::stride].unsqueeze(2).to_broadcast(shape) for n in range(2))
                w = [rt[:, n, :, 0:heads * pairs].rearrange("p t (h k) -> p t h k", k=pairs) for n in range(4)]
                for o, p, q in ((0, x1, cs), (1, x2, sn), (2, x2, cs), (3, x1, sn)):
                    for t in range(T):
                        ins = dve.tensor_tensor(w[o][:, t], p[:, t], q[:, t], ALU.mult)
                done(ins)
                for t in range(T):
                    dve.tensor_tensor(x1[:, t], w[0][:, t], w[1][:, t], ALU.subtract)
                    ins = dve.tensor_tensor(x2[:, t], w[2][:, t], w[3][:, t], ALU.add)
                done(ins)

            for l in range(DEPTH):
                lam_init = 0.8 - 0.6 * math.exp(-0.3 * l)
                for n in range(IN_P):
                    if l == 1 and n == 0:
                        layer_norm(2, x, 1)
                        turn(TURN["x3", l - 1], xT, (1,))
                    take(l, n, 1, h[:, 1, n * N:(n + 1) * N], h_dve)
                    if l == 0 and n == 1:
                        turn(TURN["mem"], memT)
                        dve.wait_ge(const_in, 16 * CONSTS)
                    if n == 1:
                        lv = lamv[:, l, :, :].rearrange("p (m two) k -> p m two k", two=2)
                        done(dve.tensor_tensor(lamp[:, :, :], lv[:, :, 0, :], lv[:, :, 1, :], ALU.mult))
                        done(dve.tensor_reduce(lams[:, 0:2], lamp[:, :, :], AX, ALU.add))
                        dve.sem_inc(lam_dots, 1)
                        done(dve.tensor_scalar(g_a[:, l, :], g_a[:, l, :], 1.0 - lam_init, None, ALU.mult))
                    if n == 2:
                        dve.wait_ge(h_act, IN_P * l + 3)
                        dve.wait_ge(trig_ready, 1)
                        rope(A_Q, 2 * 2 * AH, AQ, AQ // 8, 2)
                        rope(B_Q, 2 * BH, BD, BD // 8, 1)
                        dve.sem_inc(rope_done, 1)
                    if n == 4:
                        dve.wait_ge(lam_exps, l + 1)
                        done(dve.tensor_tensor(lams[:, 2:3], lams[:, 1:2], lams[:, 0:1], ALU.subtract))
                        done(dve.tensor_scalar(lams[:, 3:4], lams[:, 2:3], -lam_init, None, ALU.add))
                for r in (1, 3, 5):
                    b = r % 4
                    dve.wait_ge(tr_psum[b], (l if b == 3 else 2 * l + r // 4) + 1)
                    dve.tensor_copy(tr[:, 2 * r:2 * r + 2, :], ps[:, 4 + b, :].rearrange("p (b s) -> p b s", b=2))\
                        .then_inc(tr_sb[b], 1)

                def masked_max(u):
                    U = UNITS * l + u
                    dve.wait_ge(scores_ready, U + 1)
                    if u >= 2:
                        dve.wait_ge(turn_ready, U - 1)
                    for i in range(4):
                        t = u % 2 if u < 4 else i % 2
                        w = P * (t + 1)
                        m, sc = (mask_a, AQ ** -0.5) if u < 4 else (mask_b, BD ** -0.5)
                        ins = dve.scalar_tensor_tensor(s4[:, u % 2, i, 0:w], score_view(u, i), sc, m[:, t, 0:w],
                                                       ALU.mult, ALU.add)
                        if i < 3:
                            ins.then_inc(score_taken, 1)
                    done(ins)
                    dve.sem_inc(score_taken, 1)
                    if u < 4:
                        w = P * (u % 2 + 1)
                        done(dve.tensor_reduce(nmax[:, u % 2, :], s4[:, u % 2, :, 0:w], AX, ALU.max, negate=True))
                    else:
                        for t in range(T):
                            ins = dve.tensor_reduce(nmax[:, u % 2, t::2], s4[:, u % 2, t::2, 0:P * (t + 1)], AX, ALU.max,
                                                    negate=True)
                        done(ins)
                    dve.sem_inc(max_ready, 1)

                def difference(u):
                    dve.wait_ge(probs_ready, UNITS * l + u + 1)
                    rs = rsum[:, 4 * u:4 * u + 4]
                    done(dve.reciprocal(rs, sums[:, 4 * u:4 * u + 4]))
                    done(dve.tensor_scalar(rs[:, 1::2], rs[:, 1::2], lams[:, 3:4], None, ALU.mult))
                    w = P * (u % 2 + 1)
                    for j in range(2):
                        ins = dve.tensor_scalar(s4[:, u % 2, 2 * j + 1, 0:w], s4[:, u % 2, 2 * j + 1, 0:w],
                                                rs[:, 2 * j + 1:2 * j + 2], None, ALU.mult)
                    done(ins)
                    for j in range(2):
                        ins = dve.scalar_tensor_tensor(s4[:, u % 2, 2 * j, 0:w], s4[:, u % 2, 2 * j, 0:w],
                                                       rs[:, 2 * j:2 * j + 1], s4[:, u % 2, 2 * j + 1, 0:w],
                                                       ALU.mult, ALU.add)
                    ins.then_inc(diff_ready, 1)

                bc = qk[:, 1, 0, :].rearrange("p (a t s) -> p a t s", a=2, t=T)

                def level_exponents(v):
                    half = (P // 2) >> v
                    bv = qk[:, 1, 0, :].rearrange("p (n w) -> p n w", w=2 * half)
                    dve.tensor_tensor(dec[:, v, :].rearrange("p (n w) -> p n w", w=2 * half), bv,
                                      bv[:, :, half - 1:half].to_broadcast([P, 2 * S // (2 * half), 2 * half]),
                                      ALU.subtract)

                masked_max(0)
                dve.wait_ge(z_psum, l + 1)
                z3 = zz.rearrange("p a (t n) -> p a t n", t=T)
                done(dve.tensor_tensor(z3[:, 0], ps[:, 2, 0:T * CH * CK].rearrange("p (t n) -> p t n", t=T),
                                       ba[:, l, :].unsqueeze(1).to_broadcast([P, T, CH * CK]), ALU.add))
                done(dve.scalar_tensor_tensor(zz[:, 1, :], zz[:, 0, :], -1.0, zz[:, 0, :], ALU.mult, ALU.max))
                dve.sem_inc(z_abs, 1)
                oa = o_tok[:, :, 0:S].rearrange("p t (h k) -> p t h k", h=AH)
                for u in range(UNITS):
                    if u + 1 < UNITS:
                        masked_max(u + 1)
                    if u < 4:
                        difference(u)
                    if u % 2 == 0:
                        take_piece(l, u + 1)
                    if u == 0:
                        done(dve.tensor_scalar(zz[:, 0, :], zz[:, 0, :], 0.0, 1.0 / TAU, ALU.min, ALU.mult))
                        dve.wait_ge(z_ln, l + 1)
                        done(dve.tensor_scalar(zz[:, 2, :], zz[:, 1, :], -1.0 / TAU, None, ALU.mult))
                        if l == 0:
                            dve.wait_ge(pstep, 2)
                        zh = zz.rearrange("p a (t h k) -> p a t h k", t=T, h=CH)
                        for t in range(T):
                            ins = dve.tensor_tensor(cpad[:, t, 2 * CH:3 * CH, 0:CK], zh[:, 0, t], zh[:, 2, t], ALU.add)
                        ins.then_inc(decay_ready, 1)
                    if u == 1:
                        dve.wait_ge(decT_sb, l + 1)
                        for pair in range(2):
                            for t in range(T):
                                ins = dve.tensor_tensor_scan(bc[:, pair, t, :], ones, tr[:, 14 + pair, t * P:(t + 1) * P],
                                                             0.0, ALU.mult, ALU.add)
                        done(ins)
                    if 1 <= u < 4:
                        for v in (range(0, 2), range(2, 4), range(4, LEVELS))[u - 1]:
                            level_exponents(v)
                    if u == 3:
                        d7 = dec[:, 7, :].rearrange("p (a t s) -> p a t s", a=2, t=T)
                        dve.tensor_tensor(d7[:, :, 0, :], bc[:, :, 0, :], bc[:, :, 0, P - 1:P].to_broadcast([P, 2, P]),
                                          ALU.subtract)
                        done(dve.tensor_copy(d7[:, :, 1, :], bc[:, :, 1, :]))
                        dve.sem_inc(dec_diff, 1)
                    if u == 4:
                        dve.wait_ge(pv_done, UNITS * l + 4)
                        done(dve.tensor_copy(o_tok[:, :, 0:S], ps[:, 0, :].rearrange("p (t n) -> p t n", t=T)))
                        dve.sem_inc(oa_taken, 1)
                    if u == 5:
                        done(dve.tensor_tensor(oa_sq, o_tok[:, :, 0:S], o_tok[:, :, 0:S], ALU.mult))
                        done(dve.tensor_reduce(var[:, :].rearrange("p (t h) -> p t h", t=T),
                                               oa_sq.rearrange("p t (h k) -> p t h k", h=AH), AX, ALU.add))
                        norm_of(POWERS * l, 8, AV)
                    if u == 6:
                        rb = rstd[:, :].rearrange("p (t h) -> p t h", t=T).unsqueeze(3).to_broadcast([P, T, AH, AV])
                        done(dve.tensor_tensor(oa, oa, rb, ALU.mult))
                        gb = g_a[:, l, :].unsqueeze(1).to_broadcast([P, AH, AV])
                        for t in range(T):
                            dve.tensor_tensor(oa[:, t], oa[:, t], gb, ALU.mult)

                def dilated_output():
                    done(dve.reciprocal(rsum[:, 16:28], sums[:, 16:28]))
                    for t in range(T):
                        rv = rsum[:, 16 + t:28:2].unsqueeze(2).to_broadcast([P, BH, BD])
                        done(dve.tensor_tensor(o_tok[:, t, S:S + BH * BD].rearrange("p (h k) -> p h k", h=BH),
                                               ps[:, 1 - t, 0:BH * BD].rearrange("p (h k) -> p h k", h=BH), rv, ALU.mult))

                dve.wait_ge(dec_exp, l + 1)

                def products(s):
                    if s >= 3:
                        dve.wait_ge(level_scores, GSTEPS * l + s - 1)
                    for n in range(2):
                        ins = dve.tensor_tensor(qk[:, s % 2, n, :], tr[:, 10 + 2 * n:12 + 2 * n, :].rearrange("p b s -> p (b s)"),
                                                dec[:, s - 1, :], ALU.mult)
                    ins.then_inc(level_ready, 1)

                def combine(s):
                    dve.wait_ge(level_scores, GSTEPS * l + s + 1)
                    for hp in range(2):
                        src = ps[:, 4 + 2 * hp + s % 2, :].rearrange("p (b q) -> p b q", b=4)
                        if s == 0:
                            ins = dve.tensor_tensor(st[:, hp], src, ident.unsqueeze(1).to_broadcast([P, 4, P]), ALU.mult)
                        elif s <= LEVELS:
                            ins = dve.copy_predicated(st[:, hp], level[:, s - 1, :].unsqueeze(1).to_broadcast([P, 4, P]), src)
                        else:
                            ins = dve.tensor_copy(stx[:, hp], src[:, 0:2, :])
                    done(ins)
                    dve.sem_inc(level_taken, 1)

                products(1)
                dve.wait_ge(pv_done, UNITS * (l + 1))
                for s in range(GSTEPS):
                    if s + 2 < GSTEPS:
                        products(s + 2)
                    combine(s)
                    if s == 1:
                        dilated_output()
                dve.wait_ge(gla_square, l + 1)
                done(dve.tensor_reduce(var[:, :].rearrange("p (t h) -> p t h", t=T),
                                       zz[:, 0:2, :].rearrange("p t (h k) -> p t h k", h=CH), AX, ALU.add))
                norm_of(POWERS * l + 1, 8, CV, lambda: turn(TURN["k", l], kT))
                dve.wait_ge(gate_silu, l + 1)
                for t in range(T):
                    oc = o_tok[:, t, S + BH * BD:D].rearrange("p (h k) -> p h k", h=CH)
                    done(dve.tensor_tensor(oc, ps[:, 2 + t, 0:CH * CV].rearrange("p (h k) -> p h k", h=CH),
                                           rstd[:, 4 * t:4 * t + 4].unsqueeze(2).to_broadcast([P, CH, CV]), ALU.mult))
                    done(dve.tensor_tensor(oc, oc, g_c[:, l, :].unsqueeze(1).to_broadcast([P, CH, CV]), ALU.mult))
                    oc = o_tok[:, t, S + BH * BD:D]
                    done(dve.tensor_tensor(oc, oc, h[:, t, C_G:C_RANK], ALU.mult))
                    dve.sem_inc(mixed, 1)
                turn(TURN["mix", l], xT)
                out_p = IN_P + KV_P
                residual(l, out_p, 0, 0)
                residual(l, out_p, 1, 0)
                layer_norm(3 * l, x, 0)
                residual(l, out_p, 0, 1)
                residual(l, out_p, 1, 1)
                turn(TURN["x1", l], xT, (0,))
                layer_norm(3 * l, x, 1)
                turn(TURN["x1", l], xT, (1,))

                def take_q(n):
                    take(l, IN_P + KV_P + OUT_P + n, 1, q_tok[:, 1, n * N:(n + 1) * N], q_dve)

                def cross_max(t):
                    dve.wait_ge(xs_ready, T * l + t + 1)
                    banks = ps[:, 4 + 2 * t:6 + 2 * t, :].rearrange("p b (i s) -> p (b i) s", i=2)
                    done(dve.tensor_reduce(nmax[:, t, :], banks, AX, ALU.max, negate=True))
                    done(dve.tensor_scalar(nmax[:, t, :], nmax[:, t, :], XD ** -0.5, None, ALU.mult))
                    dve.sem_inc(xmax_ready, 1)

                def cross_output(t):
                    dve.wait_ge(xp_ready, T * l + t + 1)
                    done(dve.reciprocal(rsum[:, 4 * t:4 * t + 4], sums[:, 4 * t:4 * t + 4]))
                    dve.wait_ge(xo_ready, T * l + t + 1)
                    for g in range(2):
                        ins = dve.tensor_tensor(
                            o_xa[:, t, g * N:(g + 1) * N].rearrange("p (h k) -> p h k", h=2),
                            ps[:, t + 2 * g, :].rearrange("p (h k) -> p h k", h=2),
                            rsum[:, 4 * t + 2 * g:4 * t + 2 * g + 2].unsqueeze(2).to_broadcast([P, 2, XD]), ALU.mult)
                    done(ins)
                    dve.sem_inc(xo_taken, 1)

                o_p = IN_P + KV_P + OUT_P + Q_P
                turn(TURN["q", l], xT, (0,))
                take_q(0)
                cross_max(0)
                take_q(1)
                turn(TURN["q", l], xT, (1,))
                cross_output(0)
                cross_max(1)
                turn(TURN["xa", l], xT, (0,))
                residual(l, o_p, 0, 0)
                cross_output(1)
                residual(l, o_p, 1, 0)
                turn(TURN["xa", l], xT, (1,))
                layer_norm(3 * l + 1, x, 0)
                residual(l, o_p, 0, 1)
                residual(l, o_p, 1, 1)
                turn(TURN["x2", l], xT, (0,))
                layer_norm(3 * l + 1, x, 1)
                turn(TURN["x2", l], xT, (1,))
                if l == 0:
                    for n in range(FFN_CHUNKS + 1):
                        if n < FFN_CHUNKS:
                            w = min(N, F_DENSE - n * N)
                            for t in range(T):
                                u = acc_use(l, MIX_PANELS + 2 * n + 1)
                                dve.wait_ge(silu_ready, 2 * n + t + 1)
                                dve.wait_ge(acc_ready[2 + t], u // 2 + 1)
                                if n >= 2:
                                    dve.wait_ge(hT_psum[t], n - 1)
                                dve.tensor_tensor(hg[:, n % 2, t, 0:w], sg[:, t, 0:w], ps[:, 2 + t, 0:w], ALU.mult)\
                                    .then_inc(hg_ready, 1)
                                dve.wait_ge(hg_ready, 2 * n + t + 1)
                                dve.sem_inc(acc_taken[2 + t], 1)
                        if n >= 1:
                            m = n - 1
                            c = min(4, F_DENSE // P - 4 * m)
                            dve.wait_ge(hT_psum[1], m + 1)
                            dve.tensor_copy(hT[:, 4 * m:4 * m + c, P:2 * P],
                                            ps[:, 5 + 2 * (m % 2), 0:c * P].rearrange("p (c s) -> p c s", c=c))\
                                .then_inc(hT_sb[1], 1)
                    for t in range(T):
                        dve.wait_ge(w2_ready, t + 1)
                        for n in range(2):
                            xs = x[:, t, n * N:(n + 1) * N]
                            ins = dve.scalar_tensor_tensor(xs, xs, ALPHA, ps[:, 4 + 2 * t + n, :], ALU.mult, ALU.add)
                        done(ins)
                        if t == 0:
                            layer_norm(3 * l + 2, x, 0)
                    turn(TURN["x3", l], xT, (0,))

            dve.wait_ge(logit_psum, 1)
            dve.tensor_scalar(acc, x[:, :, :], ALPHA, None, ALU.mult).then_inc(acc_init, 1)
            full = [P, T, NE]

            def over(v):
                return v.unsqueeze(2).to_broadcast(full)

            done(dve.tensor_copy(lg[:, 0], ps[:, 4, 0:T * NE].rearrange("p (t e) -> p t e", t=T)))
            for c in range(2):
                done(dve.tensor_reduce(rmx[:, c, :], lg[:, c], AX, ALU.max))
                done(dve.tensor_tensor(rtmp[:, :, :], lg[:, c], over(rmx[:, c, :]), ALU.is_equal))
                done(dve.tensor_tensor(rtmp[:, :, :], rtmp[:, :, :], desc.unsqueeze(1).to_broadcast(full), ALU.mult))
                done(dve.tensor_reduce(rmx[:, 3, :], rtmp[:, :, :], AX, ALU.max))
                done(dve.tensor_tensor(oh[:, c], rtmp[:, :, :], over(rmx[:, 3, :]), ALU.is_equal))
                if c == 0:
                    done(dve.tensor_scalar(rtmp[:, :, :], oh[:, 0], -3e38, None, ALU.mult))
                    done(dve.tensor_tensor(lg[:, 1], rtmp[:, :, :], lg[:, 0], ALU.add))
            done(dve.tensor_tensor(chosen[:, :, :], oh[:, 0], oh[:, 1], ALU.add))
            dve.sem_inc(chosen_ready, 1)
            done(dve.tensor_tensor(rmx[:, 2, :], rmx[:, 1, :], rmx[:, 0, :], ALU.subtract))
            dve.sem_inc(gate_diff, 1)
            dve.wait_ge(gate_exp, 1)
            done(dve.tensor_scalar(rmx[:, 3, :], rmx[:, 2, :], 1.0, None, ALU.add))
            done(dve.reciprocal(rmx[:, 0, :], rmx[:, 3, :]))
            done(dve.tensor_tensor(rmx[:, 1, :], rmx[:, 0, :], rmx[:, 2, :], ALU.mult))
            done(dve.memset(gates[:, :, :], 0.0))
            done(dve.memset(slot[:, :, :], -1.0))
            done(dve.tensor_tensor(gates[:, :, 0:NE], oh[:, 0], over(rmx[:, 0, :]), ALU.mult))
            done(dve.tensor_tensor(rtmp[:, :, :], oh[:, 1], over(rmx[:, 1, :]), ALU.mult))
            done(dve.tensor_tensor(gates[:, :, 0:NE], gates[:, :, 0:NE], rtmp[:, :, :], ALU.add))
            dve.wait_ge(rank2_psum, 1)
            done(dve.tensor_tensor(rtmp[:, :, :], ps[:, 5, 0:T * NE].rearrange("p (t e) -> p t e", t=T), chosen[:, :, :],
                                   ALU.mult))
            done(dve.tensor_scalar(oh[:, 0], chosen[:, :, :], -1.0, 1000.0, ALU.add, ALU.mult))
            done(dve.tensor_tensor(slot[:, :, 0:NE], rtmp[:, :, :], oh[:, 0], ALU.add))
            done(dve.tensor_scalar(cnt[:, 0, :], ps[:, 5, 32:32 + NE], float(P), None, ALU.is_gt))
            done(dve.tensor_tensor_scan(cnt[:, 1, :], ones[:, 0:NE], cnt[:, 0, :], 0.0, ALU.mult, ALU.add))
            done(dve.tensor_scalar(table[:, 0:1], cnt[:, 1, NE - 1:NE], float(NE), None, ALU.add))
            done(dve.tensor_tensor(cnt[:, 2, :], cnt[:, 1, :], cnt[:, 0, :], ALU.subtract))
            for r in range(EXTRA):
                done(dve.tensor_scalar(wr[:, r, :], cnt[:, 2, :], float(r), None, ALU.is_equal))
                done(dve.tensor_tensor(wr[:, r, :], wr[:, r, :], cnt[:, 0, :], ALU.mult))
                wb = wr[:, r, :].unsqueeze(1).to_broadcast(full)
                done(dve.tensor_tensor(cnt[:, 3, :], wr[:, r, :], eid, ALU.mult))
                done(dve.tensor_reduce(table[:, r + 1:r + 2], cnt[:, 3, :], AX, ALU.add))
                done(dve.tensor_tensor(rtmp[:, :, :], gates[:, :, 0:NE], wb, ALU.mult))
                done(dve.tensor_reduce(gates[:, :, NE + r:NE + r + 1].rearrange("p t o -> p (t o)"), rtmp[:, :, :], AX, ALU.add))
                done(dve.tensor_scalar(rtmp[:, :, :], slot[:, :, 0:NE], float(P), None, ALU.subtract))
                done(dve.tensor_tensor(rtmp[:, :, :], rtmp[:, :, :], wb, ALU.mult))
                done(dve.tensor_reduce(slot[:, :, NE + r:NE + r + 1].rearrange("p t o -> p (t o)"), rtmp[:, :, :], AX, ALU.add))
            done(dve.tensor_scalar(table[:, 4:5], table[:, 0:1], -1.0, None, ALU.add))
            done(dve.tensor_copy(table_i[:, :], table[:, :]))
            dve.sem_inc(table_ready, 1)

            def select(i):
                for t in range(T):
                    ins = dve.tensor_scalar(sel[:, t, :], iota, slot[:, t, bass.ds(i, 1)], None, ALU.is_equal)
                ins.then_inc(sel_ready, 1)

            select(0)
            dve.sem_inc(he_ready, 1)
            dve.sem_inc(y_dve, 1)

            def low(q, i):
                dve.wait_ge(hi_ready, ITEM_HALVES * i + (q + 1))
                dve.tensor_tensor(w_lo[:, q % SPLIT_SLOTS, :], ring[:, q % RAW_SLOTS, :],
                                  w_hi[:, q % SPLIT_SLOTS, :].bitcast(F32), ALU.subtract).then_inc(lo_ready, 1)

            def misc_low(j, i, hi, lo, split, count):
                b = j % 2
                dve.wait_ge(split, count)
                dve.tensor_tensor(lo, ps[:, 6 + b, :].rearrange("p (c s) -> p c s", c=4), hi.bitcast(F32),
                                  ALU.subtract).then_inc(misc_taken[b], 1)

            def gather_low(i, j, g, count):
                misc_low(j + g, i, xe_hi[:, 4 * g:4 * g + 4, :], xe_lo[:, 4 * g:4 * g + 4, :], xe_split, count)

            for g in range(2):
                gather_low(0, -2, g, g + 1)
            def take_y(i):
                dve.wait_ge(y_ready, i + 1)
                dve.tensor_copy(y[:, N:D], ps[:, 5, :]).then_inc(y_dve, 1)

            def add_up(i, j):
                t, n = divmod(j - 10, 2)
                b, uses = j % 2, (2 + j) // 2
                dve.wait_ge(misc_ready[b], 7 * i + (uses + 1))
                xs = acc[:, t, n * N:(n + 1) * N]
                dve.tensor_tensor(xs, xs, ps[:, 6 + b, :], ALU.add).then_inc(misc_taken[b], 1)

            def item(i, first=False):
                for t in range(T):
                    ins = dve.tensor_scalar(gsel[:, t, :], iota, slot[:, t, bass.ds(i, 1)], gates[:, t, bass.ds(i, 1)],
                                            ALU.is_equal, ALU.mult)
                ins.then_inc(gsel_ready, 1)
                for q in range(ITEM_HALVES):
                    low(q, i)
                    if not first and q == SPLIT_SLOTS - 1:
                        take_y(i - 1)
                    if not first and q in ADDED_AT:
                        add_up(i - 1, 10 + ADDED_AT.index(q))
                    if q % 4 == 2 and 6 <= q <= 4 * MOE_PAIRS + 2:
                        n = (q - 6) // 4
                        dve.wait_ge(g_taken, MOE_PAIRS * i + (n + 2))
                        dve.wait_ge(u_ready, MOE_PAIRS * i + (n + 1))
                        if n >= 2:
                            dve.wait_ge(misc_ready[n % 2], 7 * i + (n // 2 + 1))
                        dve.tensor_tensor(hge[:, n % 2, :], sge[:, n % 2, :], ps[:, 2 * (n % 2) + 1, :], ALU.mult)\
                            .then_inc(he_ready, 1)
                    if q == 20:
                        select(i + 1)
                    if q in TURNED_AT:
                        n = TURNED_AT.index(q)
                        misc_low(n, i, he_hi[:, 4 * n:4 * n + 4, :], he_lo[:, 4 * n:4 * n + 4, :], he_split,
                                 MOE_PAIRS * i + (n + 1))
                    if q in GATHERED_AT:
                        g = GATHERED_AT.index(q)
                        gather_low(i, 7, g, 2 * i + (g + 3))

            item(0, first=True)
            n_items = dve.value_load(table_i[0:1, 0:1], min_val=NE, max_val=NE + EXTRA)
            last = dve.value_load(table_i[0:1, 4:5], min_val=NE - 1, max_val=NE + EXTRA - 1)
            with dve.Fori(1, n_items) as i:
                item(i)
            take_y(last)
            for j in range(10, 14):
                add_up(last, j)
            for b in range(2):
                dve.wait_ge(misc_taken[b], 7 * last + 8)
            for t in range(T):
                layer_norm(5, acc, t)

        @block.tensor
        def _(pe):
            def turn_tile(m, src, t):
                for g in range(2):
                    b = 2 * t + g
                    if m:
                        pe.wait_ge(tp_taken[b], m)
                    for c in range(4):
                        k = 4 * g + c
                        ins = pe.transpose(ps[:, 4 + b, c * P:(c + 1) * P], src[:, t, k * P:(k + 1) * P], ident)
                    ins.then_inc(tp_ready[b], 1)

            def turned(m, t):
                for b in (2 * t, 2 * t + 1):
                    pe.wait_ge(tp_taken[b], m + 1)

            def gemm(l, n, lhs, tiles=range(T), chunks=range(KC)):
                p, u = panel(l, n), acc_use(l, n)
                _, _, w = w_panel(l, n).shape
                rhs = slot_view(p, (P, KC, w))
                if tiles[0] == 0 and chunks[0] == 0:
                    pe.wait_ge(panel_in[p % DENSE_SLOTS], 16 * (p // DENSE_SLOTS + 1))
                for t in tiles:
                    b = 2 * (u % 2) + t
                    if u >= 2 and chunks[0] == 0:
                        pe.wait_ge(acc_taken[b], u // 2)
                    for k in chunks:
                        ins = pe.matmul(ps[:, b, 0:w], lhs[:, k, t * P:(t + 1) * P], rhs[:, k, :],
                                        start=(k == 0), stop=(k == KC - 1))
                    if chunks[-1] == KC - 1:
                        ins.then_inc(acc_ready[b], 1)
                if tiles[-1] == T - 1 and chunks[-1] == KC - 1:
                    pe.wait_ge(acc_ready[b], u // 2 + 1)
                    pe.sem_inc(panel_used, 1)

            def gemm_pair(l, n, lhs, t):
                gemm(l, n, lhs, (t,))
                gemm(l, n + 1, lhs, (t,))

            def piece(l, i, chunks=range(KC)):
                n, t = divmod(i, 2)
                p = panel(l, IN_P + n)
                if chunks[0] == 0:
                    if t == 0:
                        pe.wait_ge(panel_in[p % DENSE_SLOTS], 16 * (p // DENSE_SLOTS + 1))
                    if i == 0:
                        pe.wait_ge(acc_taken[1], acc_use(l, 4) // 2 + 1)
                    elif i <= 4 or i == 7:
                        before_ = i - 1 if i <= 4 else 5
                        pe.wait_ge((kv_act, kv_dve)[before_ % 2], KV_P * l + before_ // 2 + 1)
                rhs = slot_view(p, (P, KC, N))
                for k in chunks:
                    ins = pe.matmul(ps[:, piece_bank(i), :], memT[:, k, t * P:(t + 1) * P], rhs[:, k, :],
                                    start=(k == 0), stop=(k == KC - 1))
                if chunks[-1] == KC - 1:
                    ins.then_inc(kv_psum, 1)
                    if t == 1:
                        pe.wait_ge(kv_psum, 2 * KV_P * l + i + 1)
                        pe.sem_inc(panel_used, 1)

            pe.wait_ge(x_in, 32)
            for t in range(T):
                turn_tile(TURN["x0"], x, t)
            for t in range(T):
                turned(TURN["x0"], t)

            for l in range(DEPTH):
                if l == 0:
                    gemm_pair(l, 0, xT, 0)
                else:
                    turned(TURN["x3", l - 1], 0)
                    gemm_pair(l, 0, xT, 0)
                    pe.wait_ge(ln_done, T * 3 * l)
                    turn_tile(TURN["x3", l - 1], x, 1)
                    turned(TURN["x3", l - 1], 1)
                gemm_pair(l, 0, xT, 1)
                if l == 0:
                    pe.wait_ge(mem_in, 16)
                    for t in range(T):
                        turn_tile(TURN["mem"], o_tok, t)
                for n in range(2, IN_P):
                    gemm(l, n, xT)
                if l == 0:
                    for t in range(T):
                        turned(TURN["mem"], t)
                    pe.wait_ge(const_in, 16 * CONSTS)
                pe.wait_ge(acc_taken[0], acc_use(l, 4) // 2 + 1)
                for t in range(T):
                    for k in range(KC):
                        ins = pe.matmul(ps[:, 0, t * CR:(t + 1) * CR], xT[:, k, t * P:(t + 1) * P], w_rank[:, l, k, :],
                                        start=(k == 0), stop=(k == KC - 1))
                ins.then_inc(rank_psum, 1)

                def turn_heads(r, bank):
                    for c in range(2):
                        blk = 2 * r + c
                        for t in range(T):
                            if blk < 4:
                                src = h[:, t, blk * P:(blk + 1) * P]
                            elif blk < 10:
                                src = h[:, t, B_Q + (blk - 4) * P:B_Q + (blk - 3) * P]
                            else:
                                src = cpad[:, t, 2 * (blk - 10):2 * (blk - 9), :].rearrange("p h k -> p (h k)")
                            ins = pe.transpose(ps[:, bank, (2 * c + t) * P:(2 * c + t + 1) * P], src, ident)
                    return ins

                pe.wait_ge(rope_done, l + 1)
                for r in range(7):
                    b = r % 4
                    if r == 4:
                        pe.wait_ge(rank_sb, l + 1)
                        for t in range(T):
                            ins = pe.transpose(ps[0:CR, 0, (t + 1) * P:(t + 2) * P], rank[:, t, :], ident)
                        ins.then_inc(rankT_psum, 1)
                    if r == 5:
                        pe.wait_ge(cqk_ready, 2 * (l + 1))
                    if r >= 4:
                        pe.wait_ge(tr_sb[b], 2 * l + 1)
                    turn_heads(r, 4 + b).then_inc(tr_psum[b], 1)
                pe.wait_ge(acc_taken[2], acc_use(l, 5) // 2 + 1)
                pe.wait_ge(rankT_sb, l + 1)
                for t in range(T):
                    ins = pe.matmul(ps[:, 2, t * CH * CK:(t + 1) * CH * CK], rankT[:, t * P:(t + 1) * P], wa2[:, l, :],
                                    start=True, stop=True)
                ins.then_inc(z_psum, 1)
                for b in range(4):
                    pe.wait_ge(tr_sb[b], (2 if b < 3 else 1) * (l + 1))

                def scores(u):
                    pe.wait_ge(score_taken, 4 * (UNITS * l + u)) if u or l else None
                    for i in range(4):
                        if u < 4:
                            t, blk, r0, rn = u % 2, u // 2, AQ * i, AQ
                            q, k = tr[:, blk, :], tr[:, 2 + blk, :]
                        else:
                            t, blk, r0, rn = i % 2, u - 4, BD * (i // 2), BD
                            q, k = tr[:, 4 + blk, :], tr[:, 7 + blk, :]
                        w = P * (t + 1)
                        ins = pe.matmul(score_view(u, i), q[r0:r0 + rn, t * P:(t + 1) * P], k[r0:r0 + rn, 0:w],
                                        start=True, stop=True)
                    ins.then_inc(scores_ready, 1)

                def turn_probs(u):
                    U = UNITS * l + u
                    if u < 4:
                        pe.wait_ge(diff_ready, 4 * l + u + 1)
                    else:
                        pe.wait_ge(probs_ready, U + 1)
                    if U:
                        pe.wait_ge(turn_taken, U)
                    if u == 0:
                        pe.wait_ge(z_abs, l + 1)
                    if u == 1:
                        pe.wait_ge(decT_sb, l + 1)
                    for t in range(T):
                        if u < 4 and t != u % 2:
                            continue
                        for j in range(2):
                            src = s4[:, u % 2, 2 * j + (0 if u < 4 else t), :]
                            for kt in range(t + 1):
                                blk = j * (t + 1) + kt
                                ins = pe.transpose(ps[:, 2 + t, blk * P:(blk + 1) * P], src[:, kt * P:(kt + 1) * P], ident)
                    ins.then_inc(turn_ready, 1)

                def values(u):
                    pe.wait_ge(turn_taken, UNITS * l + u + 1)
                    if u == 4:
                        pe.wait_ge(oa_taken, l + 1)
                        pe.wait_ge(kv_act, KV_P * l + 3)
                    for t in range(T):
                        if u < 4 and t != u % 2:
                            continue
                        for j in range(2):
                            if u < 4:
                                hd = 2 * (u // 2) + j
                                o, v0 = ps[:, 0, t * S + AV * hd:t * S + AV * (hd + 1)], A_VAL + AV * hd
                            else:
                                hd = 2 * (u - 4) + j
                                o, v0 = ps[:, 1 - t, BD * hd:BD * (hd + 1)], B_VAL + BD * hd
                            for kt in range(t + 1):
                                ins = pe.matmul(o, pT[:, 2 * t + j * (t + 1) + kt, :], h[:, kt, v0:v0 + AV],
                                                start=(kt == 0), stop=(kt == t))
                    ins.then_inc(pv_done, 1)

                scores(0)
                piece(l, 0)
                for u in range(UNITS):
                    if u + 1 < UNITS:
                        scores(u + 1)
                    piece(l, u + 1, range(0, 6))
                    turn_probs(u)
                    piece(l, u + 1, range(6, KC))
                    values(u)
                    if u == 0:
                        pe.wait_ge(decay_ready, l + 1)
                        pe.wait_ge(acc_taken[3], acc_use(l, 5) // 2 + 1)
                        turn_heads(7, 3).then_inc(decT_psum, 1)

                pe.wait_ge(score_taken, 4 * UNITS * (l + 1))
                for s in range(GSTEPS):
                    if s:
                        pe.wait_ge(level_ready, (GSTEPS - 1) * l + s)
                    if s == 1:
                        pe.wait_ge(kv_act, KV_P * (l + 1))
                        pe.wait_ge(kv_dve, KV_P * (l + 1))
                    if s >= 2:
                        pe.wait_ge(level_taken, GSTEPS * l + s - 1)
                    for hp in range(2):
                        for pair in range(2):
                            for t in range(T if s <= LEVELS else 1):
                                r = slice(64 * hp, 64 * hp + 64)
                                if s == 0:
                                    q, k = tr[r, 10 + pair, :], tr[r, 12 + pair, :]
                                else:
                                    q, k = (qk[r, s % 2, n, pair * S:(pair + 1) * S] for n in range(2))
                                tq = t if s <= LEVELS else 1
                                at = (2 * pair + t if s <= LEVELS else pair) * P
                                ins = pe.matmul(ps[:, 4 + 2 * hp + s % 2, at:at + P], k[:, t * P:(t + 1) * P],
                                                q[:, tq * P:(tq + 1) * P], start=True, stop=True)
                    ins.then_inc(level_scores, 1)
                pe.wait_ge(level_taken, GSTEPS * (l + 1))
                for t in range(T):
                    for hd in range(CH):
                        pair, hp = divmod(hd, 2)
                        o = ps[:, 2 + t, CV * hd:CV * (hd + 1)]
                        v0 = C_VAL + CV * hd
                        ins = pe.matmul(o, st[:, hp, 2 * pair + t, :], h[:, t, v0:v0 + CV], start=True, stop=(t == 0))
                        if t == 1:
                            ins = pe.matmul(o, stx[:, hp, pair, :], h[:, 0, v0:v0 + CV], start=False, stop=True)
                ins.then_inc(gla_out, 1)

                for t in range(T):
                    turn_tile(TURN["k", l], k_mem, t)
                for t in range(T):
                    pe.wait_ge(mixed, T * l + t + 1)
                    turn_tile(TURN["mix", l], o_tok, t)
                for t in range(T):
                    turned(TURN["mix", l], t)
                    gemm_pair(l, IN_P + KV_P, xT, t)

                q_p = IN_P + KV_P + OUT_P
                o_p = q_p + Q_P

                def turn_q(t):
                    pe.wait_ge((q_act, q_dve)[t], Q_P * (l + 1))
                    turn_tile(TURN["q", l], q_tok, t)

                def cross_scores(t):
                    turned(TURN["q", l], t)
                    for i in range(XH):
                        for c in range(2):
                            ins = pe.matmul(cross_bank(t, i), xT[:, 2 * i + c, t * P:(t + 1) * P], kT[:, 2 * i + c, :],
                                            start=(c == 0), stop=(c == 1))
                    ins.then_inc(xs_ready, 1)

                def cross_turn(t):
                    pe.wait_ge(xp_ready, T * l + t + 1)
                    for i in range(XH):
                        for kt in range(T):
                            blk = 2 * i + kt
                            ins = pe.transpose(ps[:, 4 + 2 * t + blk // 4, (blk % 4) * P:(blk % 4 + 1) * P],
                                               s4[:, t, i, kt * P:(kt + 1) * P], ident)
                    ins.then_inc(xturn_ready, 1)

                def cross_values(t):
                    pe.wait_ge(xturn_taken, T * l + t + 1)
                    for i in range(XH):
                        for kt in range(T):
                            ins = pe.matmul(ps[:, t + 2 * (i // 2), (i % 2) * XD:(i % 2 + 1) * XD], pT[:, 2 * i + kt, :],
                                            v_mem[:, kt, i * XD:(i + 1) * XD], start=(kt == 0), stop=(kt == 1))
                    ins.then_inc(xo_ready, 1)

                def turn_xa(t):
                    pe.wait_ge(xo_taken, T * l + t + 1)
                    turn_tile(TURN["xa", l], o_xa, t)

                def turn_x(name, norm, t):
                    pe.wait_ge(ln_done, T * norm + t + 1)
                    turn_tile(TURN[name, l], x, t)

                turn_x("x1", 3 * l, 0)
                turned(TURN["x1", l], 0)
                gemm_pair(l, q_p, xT, 0)
                turn_x("x1", 3 * l, 1)
                turn_q(0)
                turned(TURN["x1", l], 1)
                gemm(l, q_p, xT, (1,))
                cross_scores(0)
                gemm(l, q_p + 1, xT, (1,))
                cross_turn(0)
                turn_q(1)
                cross_values(0)
                cross_scores(1)
                turn_xa(0)
                turned(TURN["xa", l], 0)
                gemm(l, o_p, xT, (0,))
                cross_turn(1)
                gemm(l, o_p + 1, xT, (0,), range(KC // 2))
                cross_values(1)
                gemm(l, o_p + 1, xT, (0,), range(KC // 2, KC))
                turn_xa(1)
                turned(TURN["xa", l], 1)
                gemm_pair(l, o_p, xT, 1)
                turn_x("x2", 3 * l + 1, 0)
                turned(TURN["x2", l], 0)
                if l == 0:
                    def turn_chunk(m):
                        for t in range(T):
                            pe.wait_ge(hg_ready, 2 * m + t + 1)
                            if m >= 2:
                                pe.wait_ge(hT_sb[t], m - 1)
                            for c in range(min(4, F_DENSE // P - 4 * m)):
                                ins = pe.transpose(ps[:, 4 + 2 * (m % 2) + t, c * P:(c + 1) * P],
                                                   hg[:, m % 2, t, c * P:(c + 1) * P], ident)
                            ins.then_inc(hT_psum[t], 1)

                    for n in range(FFN_CHUNKS):
                        if n == 0:
                            gemm_pair(l, MIX_PANELS, xT, 0)
                            turn_x("x2", 3 * l + 1, 1)
                            turned(TURN["x2", l], 1)
                            gemm_pair(l, MIX_PANELS, xT, 1)
                        else:
                            gemm(l, MIX_PANELS + 2 * n, xT)
                            gemm(l, MIX_PANELS + 2 * n + 1, xT)
                        if n >= 1:
                            turn_chunk(n - 1)
                    turn_chunk(FFN_CHUNKS - 1)
                    for t in range(T):
                        pe.wait_ge(hT_sb[t], FFN_CHUNKS)

                    def w2(j, t):
                        p = panel(l, MIX_PANELS + 2 * FFN_CHUNKS + j)
                        shape = w_panel(l, MIX_PANELS + 2 * FFN_CHUNKS + j).shape
                        rhs = slot_view(p, shape)
                        if t == 0:
                            pe.wait_ge(panel_in[p % DENSE_SLOTS], 16 * (p // DENSE_SLOTS + 1))
                        for g in range(2):
                            for c in range(shape[1]):
                                k = 4 * j + c
                                ins = pe.matmul(ps[:, 4 + 2 * t + g, :], hT[:, k, t * P:(t + 1) * P],
                                                rhs[:, c, g * N:(g + 1) * N], start=(k == 0),
                                                stop=(k == F_DENSE // P - 1))
                        return ins

                    for j in range(W2_P - 2):
                        for t in range(T):
                            ins = w2(j, t)
                        ins.then_inc(panel_used, 1)
                    for t in range(T):
                        ins = w2(W2_P - 2, t)
                        if t == 1:
                            ins.then_inc(panel_used, 1)
                        w2(W2_P - 1, t).then_inc(w2_ready, 1)
                    pe.wait_ge(w2_ready, T)
                    pe.sem_inc(panel_used, 1)
                    turn_x("x3", 3 * l + 2, 0)
                else:
                    turn_x("x2", 3 * l + 1, 1)
                    turned(TURN["x2", l], 1)

            for t in range(T):
                for k in range(KC):
                    ins = pe.matmul(ps[:, 4, t * NE:(t + 1) * NE], xT[:, k, t * P:(t + 1) * P], w_router[:, k, :],
                                    start=(k == 0), stop=(k == KC - 1))
            ins.then_inc(logit_psum, 1)
            pe.wait_ge(chosen_ready, 1)
            pe.matmul(ps[:, 5, 0:NE], before, chosen[:, 0, :], start=True, stop=True)
            pe.matmul(ps[:, 5, NE:2 * NE], before, chosen[:, 1, :], start=True, stop=False)
            pe.matmul(ps[:, 5, NE:2 * NE], ones, chosen[:, 0, :], start=False, stop=True)
            pe.matmul(ps[:, 5, 32:32 + NE], ones, chosen[:, 0, :], start=True, stop=False)
            pe.matmul(ps[:, 5, 32:32 + NE], ones, chosen[:, 1, :], start=False, stop=True).then_inc(rank2_psum, 1)

            def misc_bank(j, i):
                q = 2 + j
                b, uses = q % 2, q // 2
                if j >= 0:
                    pe.wait_ge(misc_taken[b], 7 * i + uses)
                return b

            def gather(i, j, count):
                pe.wait_ge(sel_ready, count)
                for g in range(2):
                    b = misc_bank(j + g, i)
                    for c in range(4):
                        for t in range(T):
                            k = 4 * g + c
                            ins = pe.matmul(ps[:, 6 + b, c * P:(c + 1) * P], x[:, t, k * P:(k + 1) * P], sel[:, t, :],
                                            start=(t == 0), stop=(t == T - 1))
                    ins.then_inc(misc_ready[b], 1)

            def turn_item(n, i, j):
                pe.wait_ge(he_ready, MOE_PAIRS * i + (n + 2))
                b = misc_bank(j, i)
                for c in range(4):
                    ins = pe.transpose(ps[:, 6 + b, c * P:(c + 1) * P], hge[:, n % 2, c * P:(c + 1) * P], ident)
                ins.then_inc(misc_ready[b], 1)

            gather(0, -2, 1)
            pe.sem_inc(half_used, SPLIT_SLOTS)
            pe.wait_ge(table_ready, 1)
            def product(q, bank, x_hi, x_lo, c, cols, first, last):
                hi, lo = half_view(w_hi, q, SPLIT_SLOTS), half_view(w_lo, q, SPLIT_SLOTS)
                pe.matmul(ps[:, bank, :], x_hi, hi[:, c, cols], start=first, stop=False)
                pe.matmul(ps[:, bank, :], x_hi, lo[:, c, cols], start=False, stop=False)
                return pe.matmul(ps[:, bank, :], x_lo, hi[:, c, cols], start=False, stop=last)

            def scatter(i):
                pe.wait_ge(misc_taken[1], 7 * i + 6)
                pe.wait_ge(y_act, i + 2)
                pe.wait_ge(y_dve, i + 2)
                for t in range(T):
                    for n in range(2):
                        b = misc_bank(10 + 2 * t + n, i)
                        pe.matmul(ps[:, 6 + b, :], gselT[:, t * P:(t + 1) * P], y[:, n * N:(n + 1) * N],
                                  start=True, stop=True).then_inc(misc_ready[b], 1)

            def item(i, first=False):
                if first:
                    for b in range(2):
                        pe.wait_ge(misc_taken[b], 1)
                for q in range(4 * MOE_PAIRS):
                    n, g, r = q // 4, q // 2 % 2, q % 2
                    ready, taken = ((g_ready, g_taken), (u_ready, he_ready))[g]
                    pe.wait_ge(lo_ready, ITEM_HALVES * i + (q + 1))
                    if r == 0 and n >= 2:
                        pe.wait_ge(taken, MOE_PAIRS * i + n)
                    elif r == 0 and n == 0:
                        pe.wait_ge(taken, MOE_PAIRS * i + 1)
                    for c in range(4):
                        k = 4 * r + c
                        ins = product(q, 2 * (n % 2) + g, xe_hi[:, k, :], xe_lo[:, k, :], c, slice(0, N),
                                      k == 0, k == KC - 1)
                    ins.then_inc(half_used, 1)
                    if r == 1:
                        pe.wait_ge(half_used, ITEM_HALVES * i + (q + 1 + SPLIT_SLOTS))
                        pe.sem_inc(ready, 1)
                    if q == 4 and not first:
                        scatter(i - 1)
                    if q % 4 == 3 and n >= 1:
                        turn_item(n - 1, i, n - 1)
                for q in range(4 * MOE_PAIRS, ITEM_HALVES):
                    jj, r = divmod(q - 4 * MOE_PAIRS, 2)
                    pe.wait_ge(lo_ready, ITEM_HALVES * i + (q + 1))
                    if q == 4 * MOE_PAIRS:
                        pe.wait_ge(y_act, i + 1)
                        pe.wait_ge(y_dve, i + 1)
                    if r == 0:
                        pe.wait_ge(misc_taken[jj % 2], 7 * i + (jj // 2 + 2))
                    for g in range(2):
                        for c in range(2):
                            k = 4 * jj + 2 * r + c
                            ins = product(q, 4 + g, he_hi[:, k, :], he_lo[:, k, :], c, slice(g * N, (g + 1) * N),
                                          k == 0, k == 4 * MOE_PAIRS - 1)
                    ins.then_inc(half_used, 1)
                    if q == 31:
                        turn_item(6, i, 6)
                    if q == 33:
                        gather(i, 7, i + 2)
                    if q == 37:
                        pe.wait_ge(gsel_ready, i + 1)
                        b = misc_bank(9, i)
                        for t in range(T):
                            ins = pe.transpose(ps[:, 6 + b, t * P:(t + 1) * P], gsel[:, t, :], ident)
                        ins.then_inc(misc_ready[b], 1)
                pe.wait_ge(half_used, ITEM_HALVES * (i + 1) + SPLIT_SLOTS)
                pe.sem_inc(y_ready, 1)
                for b in range(2):
                    pe.wait_ge(misc_taken[b], 7 * i + (6 - b))

            item(0, first=True)
            n_items = pe.value_load(table_i[0:1, 0:1], min_val=NE, max_val=NE + EXTRA)
            last = pe.value_load(table_i[0:1, 4:5], min_val=NE - 1, max_val=NE + EXTRA - 1)
            with pe.Fori(1, n_items) as i:
                item(i)
            scatter(last)


_INS = ["x", "mem", "positions", "w_in", "lam_q1", "lam_k1", "lam_q2", "lam_k2", "diff_norm_g", "gla_wa2", "gla_ba",
        "gla_norm_g", "w_out", "ln_mix_g", "ln_mix_b", "xa_wq", "xa_wkv", "xa_wo", "ln_xa_g", "ln_xa_b",
        "ffd_w13", "ffd_w2", "moe_router", "moe_w13", "moe_w2", "ln_ffn_g", "ln_ffn_b"]


def kernel(**inputs):
    import concourse.bacc as bacc
    from concourse.bass_utils import run_bass_kernel_spmd as run

    nc = bacc.Bacc("TRN2", target_bir_lowering=False, num_devices=1)
    given = {name: np.ascontiguousarray(inputs[name]) for name in _INS}
    given.update(shape_constants())
    arrays, args = {}, {}
    for name, value in given.items():
        arrays[f"in_{name}_dram"] = value
        args[name] = nc.dram_tensor(f"in_{name}_dram", value.shape, mybir.dt.from_np(value.dtype),
                                    kind="ExternalInput").ap()
    result = nc.dram_tensor("out_0_dram", (1, S, D), F32, kind="ExternalOutput").ap()
    bass_decoder(nc, args, result)
    r = run(nc, [arrays], core_ids=[0])
    return r.results[0]["out_0_dram"]
```

```python
import math
from contextlib import ExitStack

import numpy as np
import concourse.bass as bass
from concourse import mybir

F32 = mybir.dt.float32
I32 = mybir.dt.int32
F32R = mybir.dt.float32r
ALU = mybir.AluOpType
ACT = mybir.ActivationFunctionType
AX = mybir.AxisListType.X

P = 128
D = 1024
S = 256
T = S // P
KC = D // P
N = 512
DEPTH = 2
ALPHA = (2 * DEPTH) ** 0.25
EPS = 1e-5
NEG = -1e30
THETA = 500000.0

AH, AQ, AV = 4, 32, 64
BH, BD = 6, 64
CH, CK, CV, CR = 4, 48, 96, 16
TAU = 16.0
XH, XD = 4, 256
A_Q, A_K, A_VAL = 0, 256, 512
B_Q, B_K, B_VAL = 768, 1152, 1536
C_Q, C_K, C_VAL, C_G, C_RANK = 1920, 2112, 2304, 2688, 3072
IN_COLS = 3088
F_DENSE = 2816
NE, F_MOE = 8, 3584
EXTRA = 3
ROPE = 8

RAW_SLOTS = 7
DENSE_SLOTS = 5
SPLIT_SLOTS = 3
HALF = KC * N // 2
IN_P, KV_P, OUT_P, Q_P, O_P = 6, 4, 2, 2, 2
MIX_PANELS = IN_P + KV_P + OUT_P + Q_P + O_P
FFN_CHUNKS = -(-F_DENSE // N)
W2_P = -(-(F_DENSE // P) // 4)
L1 = MIX_PANELS + 2 * FFN_CHUNKS + W2_P
L1_ACC = MIX_PANELS - KV_P + 2 * FFN_CHUNKS

DENSE_HALVES = [(l, n, g) for l in range(DEPTH) for n in range(L1 if l == 0 else MIX_PANELS)
                for g in range(1 if n == L1 - 1 else 2)]
SPLIT_HALVES = [(l, n, g) for l, n, g in DENSE_HALVES
                if n < IN_P or n >= MIX_PANELS or 0 <= n - (IN_P + KV_P + OUT_P) < Q_P]
HALF_AT = {name: i for i, name in enumerate(DENSE_HALVES)}
SPLIT_AT = {name: i for i, name in enumerate(SPLIT_HALVES)}
HIGH_SLOTS = 4
MOE_PAIRS = F_MOE // N
ITEM_HALVES = 6 * MOE_PAIRS
UNITS = 7
TURNED_AT = [4 * n + 11 for n in range(MOE_PAIRS - 1)] + [35]
GATHERED_AT = [37, 38]
SCATTERED_AT = [3, 4, 5, 6]
ADDED_AT = [7, 8, 9, 10]
EXTRAS_AT = [8, 11, 15, 19, 23]
LEVELS = 7
GSTEPS = LEVELS + 2
MAGIC = 1.5 * 2.0 ** 23
PI2 = (6.28125, 0.0019350051879882812, 3.0198e-07)


def shape_constants():
    i = np.arange(P)
    q = np.arange(S).reshape(T, P).T
    k = np.arange(S)
    dist = q[:, :, None] - k[None, None, :]
    mask_a = np.where(dist >= 0, 0.0, NEG).astype(np.float32)
    times = ((dist >= 0) & (dist <= 128)).astype(np.int64)
    for dilation in (4, 16):
        times = times + ((dist >= 0) & (dist % dilation == 0))
    mask_b = np.where(times > 0, np.log(np.maximum(times, 1)), NEG).astype(np.float32)
    level = np.zeros((P, LEVELS, P), np.int32)
    for v in range(LEVELS):
        half = (P // 2) >> v
        block = i // (2 * half)
        upper = (i // half) % 2
        level[:, v, :] = (block[:, None] == block[None, :]) & (upper[:, None] == 0) & (upper[None, :] == 1)
    square = np.stack([np.eye(P), i[:, None] < i[None, :], np.ones((P, P)),
                       np.broadcast_to(i[None, :], (P, P))], 1).astype(np.float32)
    freq = (THETA ** (-np.arange(0, 2 * ROPE, 2, dtype=np.float32) / np.float32(2 * ROPE))).astype(np.float32)
    e = np.arange(NE, dtype=np.float32)
    rows = np.concatenate([freq, NE - e, e, np.arange(EXTRA, dtype=np.float32)])
    rows = np.broadcast_to(rows[None, :], (P, rows.size)).astype(np.float32)
    return {"mask_a": mask_a, "mask_b": mask_b, "level": level, "square": square,
            "rows": np.ascontiguousarray(rows)}


def bass_decoder(nc, a, out):
    ctx = ExitStack()
    with ctx:
        def sb(name, shape, dt=F32):
            return ctx.enter_context(nc.sbuf_tensor(name, shape, dt))

        def sem(name):
            return ctx.enter_context(nc.semaphore(name))

        with ExitStack() as scope:
            ring_r = scope.enter_context(nc.sbuf_tensor("ring_r", [P, RAW_SLOTS, HALF], F32R))
        ring = sb("ring", [P, RAW_SLOTS, HALF])
        ringf = ring[:, :, :].rearrange("p s n -> p (s n)")
        x = sb("x", [P, T, D])
        ln_gb = sb("ln_gb", [P, 2, D])
        square = sb("square", [P, 4, P])
        ident, before, ones, iota = (square[:, n, :] for n in range(4))
        rows = sb("rows", [P, ROPE + 2 * NE + EXTRA])
        freq = rows[:, 0:ROPE]
        desc = rows[:, ROPE:ROPE + NE]
        eid = rows[:, ROPE + NE:ROPE + 2 * NE]
        w_router = sb("w_router", [P, KC, NE])
        stats = sb("stats", [P, T, 2, 6])
        mv = sb("mv", [P, T, 2])
        var = sb("var", [P, 8])
        rstd = sb("rstd", [P, 8])
        mhalf = sb("mhalf", [P, 8])
        lg = sb("lg", [P, 2, T, NE])
        oh = sb("oh", [P, 2, T, NE])
        rtmp = sb("rtmp", [P, T, NE])
        rmx = sb("rmx", [P, 4, T])
        chosen = sb("chosen", [P, T, NE])
        gates = sb("gates", [P, T, 12])
        slot = sb("slot", [P, T, 12])
        cnt = sb("cnt", [P, 4, NE])
        wr = sb("wr", [P, EXTRA, NE])
        table = sb("table", [P, 5])
        table_i = sb("table_i", [P, 5], I32)

        with ExitStack() as scope:
            def sbe(name, shape, dt=F32):
                return scope.enter_context(nc.sbuf_tensor(name, shape, dt))

            w_hi = sbe("w_hi", [P, SPLIT_SLOTS, HALF], F32R)
            w_lo = sbe("w_lo", [P, SPLIT_SLOTS, HALF], F32R)
            he_hi = sbe("he_hi", [P, F_MOE // P, P], F32R)
            he_lo = sbe("he_lo", [P, F_MOE // P, P], F32R)
            xe_hi = sbe("xe_hi", [P, KC, P], F32R)
            xe_lo = sbe("xe_lo", [P, KC, P], F32R)
            accum = sbe("accum", [P, T, D])
            acc = accum[:, :, :]
            y = sbe("y", [P, D])
            sge = sbe("sge", [P, 2, N])
            hge = sbe("hge", [P, 2, N])
            sel = sbe("sel", [P, T, P])
            gsel = sbe("gsel", [P, T, P])
            gselT = sbe("gselT", [P, T * P])

        with ExitStack() as scope:
            def twin(name, shape):
                return scope.enter_context(nc.sbuf_tensor(name, shape, F32R))

            late_r = twin("late_r", [P, 4 * KC * N])[:, :]
            xT_r = twin("xT_r", [P, KC, S])
            twin("memT_r", [P, KC, S])
            h_r = twin("h_r", [P, T, IN_COLS])
            twin("cpad_r", [P, T, 3 * CH, 64])
            qk_r = twin("qk_r", [P, 2, 2, 2 * S])
        late = sb("late", [P, 4 * KC * N])[:, :]
        xT = sb("xT", [P, KC, S])
        tr = late[:, 0:4096].rearrange("p (b s) -> p b s", b=16)
        kT = late[:, 4096:6144].rearrange("p (c s) -> p c s", c=KC)
        v_mem = late[:, 6144:8192].rearrange("p (t d) -> p t d", t=T)
        o_tok = late[:, 8192:10240].rearrange("p (t d) -> p t d", t=T)
        dec = late[:, 10240:14336].rearrange("p (v n) -> p v n", v=8)
        s4 = late[:, 14336:16384].rearrange("p (b i k) -> p b i k", b=2, i=4)
        hg = dec[:, 0:4, :].rearrange("p (b t) n -> p b t n", b=2)
        x_hi = xT_r[:, :, :]
        x_low = late[:, 0:2048].rearrange("p (c s) -> p c s", c=KC)
        x_lo = late_r[:, 0:2048].rearrange("p (c s) -> p c s", c=KC)
        pT_cross = dec[:, 0:2, :].rearrange("p v (c s) -> p (v c) s", c=4)
        mem_tok = late[:, 6144:8192].rearrange("p (t d) -> p t d", t=T)
        sg = s4[:, 0, :, :].rearrange("p i k -> p (i k)").rearrange("p (t n) -> p t n", t=T)
        k_mem = xT[:, :, :].rearrange("p c s -> p (c s)").rearrange("p (t d) -> p t d", t=T)
        memT = sb("memT", [P, KC, S])
        h = sb("h", [P, T, IN_COLS])
        hflat = h[:, :, :].rearrange("p t n -> p (t n)")
        h_hi = h_r[:, :, :].rearrange("p t n -> p (t n)")[:, 0:F_DENSE // P * S].rearrange("p (c s) -> p c s", s=S)
        h_lo = late_r[:, 2048:2048 + F_DENSE // P * S].rearrange("p (c s) -> p c s", s=S)
        q_tok = h[:, :, 0:D]
        o_xa = h[:, :, D:2 * D]
        cpad = sb("cpad", [P, T, 3 * CH, 64])
        qk = sb("qk", [P, 2, 2, 2 * S])
        spare = ring[:, RAW_SLOTS - 1, :]
        st = spare[:, 0:8 * P].rearrange("p (h b s) -> p h b s", h=2, b=4)
        stx = spare[:, 8 * P:12 * P].rearrange("p (h b s) -> p h b s", h=2, b=2)
        high = (ring_r[:, DENSE_SLOTS, :], late_r[:, 8192:10240], late_r[:, 12288:14336],
                qk_r[:, :, :, :].rearrange("p m n s -> p (m n s)"))
        pT = qk[:, 0, :, :].rearrange("p n s -> p (n s)").rearrange("p (c s) -> p c s", c=8)
        mask_a = sb("mask_a", [P, T, S])
        mask_b = sb("mask_b", [P, T, S])
        level = sb("level", [P, LEVELS, P], I32)
        lamv = sb("lamv", [P, DEPTH, 4, AQ])
        g_a = sb("g_a", [P, DEPTH, AV])
        g_c = sb("g_c", [P, DEPTH, CV])
        ba = sb("ba", [P, DEPTH, CH * CK])
        wa2 = sb("wa2", [CR, DEPTH, CH * CK])
        w_rank = spare[:, 12 * P:14 * P].rearrange("p (l c r) -> p l c r", l=DEPTH, c=KC)
        pos_i = sb("pos_i", [P, T], I32)
        pos = sb("pos", [P, T])
        ang = sb("ang", [P, 2, T, ROPE])
        angr = sb("angr", [P, 2, T, ROPE])
        trig = sb("trig", [P, 2, T, ROPE])
        rt = s4[:, 0, :, 0:T * 24 * 4].rearrange("p n (t k) -> p n t k", t=T)
        wr_hi, wr_lo = (ring_r[:, RAW_SLOTS - 1, m * KC * CR:(m + 1) * KC * CR].rearrange("p (c r) -> p c r", c=KC)
                        for m in range(2))
        rankT = spare[0:CR, 14 * P:16 * P]
        zz = dec[:, 0:3, 0:T * CH * CK]
        oa_sq = spare[:, 0:T * S].rearrange("p (t n) -> p t n", t=T)
        lamp = sb("lamp", [P, 2, AQ])
        lams = sb("lams", [P, 4])
        nmax = sb("nmax", [P, 2, 4])
        sums = sb("sums", [P, 4 * UNITS])
        rsum = sb("rsum", [P, 4 * UNITS])

        ps = ctx.enter_context(nc.psum_tensor("ps", [P, 8, N], F32))

        x_in, mem_in = sem("x_in"), sem("mem_in")
        pos_in, const_in = sem("pos_in"), sem("const_in")
        ln_in = sem("ln_in")
        dense_in = [sem(f"dense_in{s}") for s in range(DENSE_SLOTS)]
        dense_used = sem("dense_used")
        dense_hi, dense_lo = sem("dense_hi"), sem("dense_lo")
        x_split, h_split = sem("x_split"), sem("h_split")
        acc_ready = [sem(f"acc_ready{b}") for b in range(4)]
        acc_taken = [sem(f"acc_taken{b}") for b in range(4)]
        tp_ready = [sem(f"tp_ready{b}") for b in range(4)]
        tp_taken = [sem(f"tp_taken{b}") for b in range(4)]
        h_act, h_dve = sem("h_act"), sem("h_dve")
        kv_psum = sem("kv_psum")
        kv_act, kv_dve = sem("kv_act"), sem("kv_dve")
        q_act, q_dve = sem("q_act"), sem("q_dve")
        wr_high, wr_ready = sem("wr_high"), sem("wr_ready")
        rankT_psum, rankT_sb = sem("rankT_psum"), sem("rankT_sb")
        z_psum, z_abs, z_ln = sem("z_psum"), sem("z_abs"), sem("z_ln")
        angles, trig_ready = sem("angles"), sem("trig_ready")
        lam_dots, lam_exps = sem("lam_dots"), sem("lam_exps")
        rope_done = sem("rope_done")
        cqk_ready, decay_ready = sem("cqk_ready"), sem("decay_ready")
        tr_psum = [sem(f"tr_psum{b}") for b in range(4)]
        tr_sb = [sem(f"tr_sb{b}") for b in range(4)]
        decT_psum, decT_sb = sem("decT_psum"), sem("decT_sb")
        gate_silu = sem("gate_silu")
        scores_ready, score_taken = sem("scores_ready"), sem("score_taken")
        max_ready, probs_ready, diff_ready = sem("max_ready"), sem("probs_ready"), sem("diff_ready")
        turn_ready, turn_taken, pv_done = sem("turn_ready"), sem("turn_taken"), sem("pv_done")
        oa_taken = sem("oa_taken")
        dec_diff, dec_exp = sem("dec_diff"), sem("dec_exp")
        level_ready, level_scores, level_taken = sem("level_ready"), sem("level_scores"), sem("level_taken")
        gla_out, gla_square = sem("gla_out"), sem("gla_square")
        mixed = sem("mixed")
        xs_ready, xmax_ready, xp_ready = sem("xs_ready"), sem("xmax_ready"), sem("xp_ready")
        xturn_ready, xturn_taken = sem("xturn_ready"), sem("xturn_taken")
        xo_ready, xo_taken = sem("xo_ready"), sem("xo_taken")
        var_ready, rstd_ready = sem("var_ready"), sem("rstd_ready")
        ln_done = sem("ln_done")
        silu_ready, hg_ready = sem("silu_ready"), sem("hg_ready")
        hT_psum = [sem(f"hT_psum{t}") for t in range(T)]
        hT_sb = [sem(f"hT_sb{t}") for t in range(T)]
        w2_ready = sem("w2_ready")
        logit_psum, chosen_ready, rank2_psum = sem("logit_psum"), sem("chosen_ready"), sem("rank2_psum")
        gate_diff, gate_exp = sem("gate_diff"), sem("gate_exp")
        table_ready = sem("table_ready")
        raw_in = [sem(f"raw_in{s}") for s in range(RAW_SLOTS)]
        hi_ready, lo_ready = sem("hi_ready"), sem("lo_ready")
        half_used = sem("half_used")
        he_split, xe_split = sem("he_split"), sem("xe_split")
        sel_ready, gsel_ready = sem("sel_ready"), sem("gsel_ready")
        g_taken, he_ready = sem("g_taken"), sem("he_ready")
        misc_ready = [sem(f"misc_ready{b}") for b in range(2)]
        misc_taken = [sem(f"misc_taken{b}") for b in range(2)]
        y_act, y_dve = sem("y_act"), sem("y_dve")
        acc_init = sem("acc_init")
        out_done = sem("out_done")
        vstep = sem("vstep")
        sstep = sem("sstep")
        pstep = sem("pstep")

        CONSTS = 14
        POWERS = 2 + 3 * T
        TURN = {"x0": 0, "mem": 1}
        for l in range(DEPTH):
            for n, name in enumerate(("k", "mix", "x1", "q", "xa", "x2", "x3")):
                TURN[name, l] = 2 + 7 * l + n

        def acc_use(l, n):
            return l * L1_ACC + (n if n < IN_P else n - KV_P)

        def w_panel(l, n):
            def cols(w, c0, width=N):
                return w.rearrange("(c p) n -> p c n", p=P)[:, :, c0:c0 + width]
            for w, count in ((a["w_in"][l], IN_P), (a["xa_wkv"][l], KV_P), (a["w_out"][l], OUT_P),
                             (a["xa_wq"][l], Q_P), (a["xa_wo"][l], O_P)):
                if n < count:
                    return cols(w, n * N)
                n -= count
            if n < 2 * FFN_CHUNKS:
                width = min(N, F_DENSE - n // 2 * N)
                return cols(a["ffd_w13"][0], (n % 2) * F_DENSE + n // 2 * N, width)
            n -= 2 * FFN_CHUNKS
            r0, r1 = 4 * n, min(4 * n + 4, F_DENSE // P)
            return a["ffd_w2"][0].rearrange("(c p) n -> p c n", p=P)[:, r0:r1, :]

        def dense_src(l, n, g):
            src = w_panel(l, n)
            c = 2 if n >= L1 - W2_P else 4
            return src[:, c * g:c * (g + 1), :]

        def dense_view(buffer, l, n, g):
            _, c, w = dense_src(l, n, g).shape
            return buffer[:, 0:c * w].rearrange("p (c n) -> p c n", c=c)

        def raw_half(l, n, g):
            return dense_view(ring[:, HALF_AT[l, n, g] % DENSE_SLOTS, :], l, n, g)

        def high_half(l, n, g):
            return dense_view(high[SPLIT_AT[l, n, g] % HIGH_SLOTS], l, n, g)

        def low_half(l, n, g):
            return dense_view(ring_r[:, HALF_AT[l, n, g] % DENSE_SLOTS, :], l, n, g)

        def half_view(buffer, q, slots):
            return buffer[:, q % slots, :].rearrange("p (c n) -> p c n", c=4 if q < 4 * MOE_PAIRS else 2)

        def piece_bank(i):
            return 1 if i <= 4 else 5 if i % 2 else 7

        def score_view(u, i):
            if u < 4:
                return ps[:, 4 + i, 0:P * (u % 2 + 1)]
            j, t = divmod(i, 2)
            return ps[:, 4 + 2 * j, P * t:P * (2 * t + 1)]

        def wait_used(engine, index):
            l, n, g = DENSE_HALVES[index]
            if n == L1 - 1:
                engine.wait_ge(w2_ready, T)
            elif g == 0 or n >= L1 - W2_P:
                own = sum(1 for m, k, c in DENSE_HALVES[:index + 1] if (c == 0 or k >= L1 - W2_P) and k != L1 - 1)
                engine.wait_ge(dense_used, own)
            elif IN_P <= n < IN_P + KV_P:
                engine.wait_ge(kv_psum, 2 * KV_P * l + 2 * (n - IN_P) + 2)
            else:
                u = acc_use(l, n)
                engine.wait_ge(acc_ready[2 * (u % 2) + 1], u // 2 + 1)

        def cross_bank(t, i):
            return ps[:, 4 + 2 * t + i // 2, i % 2 * S:(i % 2 + 1) * S]

        block = ctx.enter_context(nc.Block())

        @block.sync
        def _(sp):
            sp.dma_start(x[:, :, :], a["x"][0].rearrange("(t p) d -> p t d", p=P)).then_inc(x_in, 16)
            sp.dma_start(square[:, :, :], a["square"]).then_inc(x_in, 16)

            def load_ln(k):
                l, s = divmod(k, 3)
                g, b = (("ln_mix_g", "ln_mix_b"), ("ln_xa_g", "ln_xa_b"), ("ln_ffn_g", "ln_ffn_b"))[s]
                if k:
                    sp.wait_ge(ln_done, T * k)
                for n, w in enumerate((g, b)):
                    sp.dma_start(ln_gb[:, n, :], a[w][l:l + 1, :].to_broadcast([P, D])).then_inc(ln_in, 16)

            def dense(l, n):
                for g in range(1 if n == L1 - 1 else 2):
                    at = HALF_AT[l, n, g]
                    if at >= DENSE_SLOTS:
                        wait_used(sp, at - DENSE_SLOTS)
                    sp.dma_start(raw_half(l, n, g), dense_src(l, n, g)).then_inc(dense_in[at % DENSE_SLOTS], 16)

            for l in range(DEPTH):
                for n in range(L1 if l == 0 else MIX_PANELS):
                    dense(l, n)
                    if l == 0 and n == 1:
                        sp.dma_start(mem_tok, a["mem"][0].rearrange("(t p) d -> p t d", p=P)).then_inc(mem_in, 16)
                    if n == IN_P + KV_P + OUT_P - 1:
                        load_ln(3 * l)
                    if n == MIX_PANELS - 1:
                        load_ln(3 * l + 1)
                    if n == L1 - 1:
                        load_ln(3 * l + 2)

            def item_half(q, i, e):
                if q < 4 * MOE_PAIRS:
                    c0 = (q // 2 % 2) * F_MOE + q // 4 * N
                    r = 4 * (q % 2)
                    src = a["moe_w13"][0, e].rearrange("(c p) n -> p c n", p=P)[:, r:r + 4, c0:c0 + N]
                else:
                    r = 2 * (q - 4 * MOE_PAIRS)
                    src = a["moe_w2"][0, e].rearrange("(c p) n -> p c n", p=P)[:, r:r + 2, :]
                sp.dma_start(half_view(ring, q, RAW_SLOTS), src).then_inc(raw_in[q % RAW_SLOTS], 16)

            def item_halves(i, e, first=0):
                for q in range(first, ITEM_HALVES):
                    sp.wait_ge(lo_ready, ITEM_HALVES * i + (q - RAW_SLOTS + 1))
                    item_half(q, i, e)

            for q in range(RAW_SLOTS - 1):
                if q < DENSE_SLOTS:
                    last = max(i for i in range(len(DENSE_HALVES)) if i % DENSE_SLOTS == q)
                    wait_used(sp, last)
                item_half(q, 0, 0)
            load_ln(5)
            item_half(RAW_SLOTS - 1, 0, 0)
            item_halves(0, 0, RAW_SLOTS)
            with sp.Fori(1, NE) as i:
                item_halves(i, i)
            sp.wait_ge(table_ready, 1)
            n_items = sp.value_load(table_i[0:1, 0:1], min_val=NE, max_val=NE + EXTRA)
            with sp.If(n_items > NE):
                with sp.Fori(NE, n_items) as i:
                    e = sp.value_load(table_i[0:1, bass.ds(i - (NE - 1), 1)], min_val=0, max_val=NE - 1)
                    item_halves(i, e)
            sp.wait_ge(ln_done, T * 6)
            sp.dma_start(out[0].rearrange("(t p) d -> p t d", p=P), acc).then_inc(out_done, 16)
            sp.wait_ge(out_done, 16)

        @block.gpsimd
        def _(pool):
            pool.memset(mhalf[:, :], -0.5).then_inc(pstep, 1)
            pool.memset(cpad[:, :, :, CK:64], 0.0).then_inc(pstep, 1)
            pool.wait_ge(pstep, 2)
            for k in range(POWERS * DEPTH):
                c = slice(0, 8) if k % POWERS < 2 else slice(k % 2, k % 2 + 1)
                pool.wait_ge(var_ready, k + 1)
                pool.tensor_tensor(rstd[:, c], var[:, c], mhalf[:, c], ALU.pow).then_inc(rstd_ready, 1)

        @block.scalar
        def _(act):
            step = [0]

            def done(ins):
                step[0] += 1
                ins.then_inc(sstep, 1)
                act.wait_ge(sstep, step[0])

            def take(l, n, t, dst, signal):
                u = acc_use(l, n)
                b = 2 * (u % 2) + t
                act.wait_ge(acc_ready[b], u // 2 + 1)
                act.copy(dst, ps[:, b, :]).then_inc(signal, 1)
                act.wait_ge(signal, signal_count[signal.name] + 1)
                signal_count[signal.name] += 1
                act.sem_inc(acc_taken[b], 1)

            signal_count = {h_act.name: 0, q_act.name: 0}

            def turn(m, dst, tiles=range(T)):
                for t in tiles:
                    b = 2 * t
                    act.wait_ge(tp_ready[b], m + 1)
                    act.copy(dst[:, 0:4, t * P:(t + 1) * P],
                             ps[:, 4 + b, :].rearrange("p (c s) -> p c s", c=4)).then_inc(tp_taken[b], 1)

            dense_splits = [0]

            def turn_split(m, tiles=range(T)):
                for t in tiles:
                    for g in range(2):
                        act.wait_ge(tp_ready[2 * t + g], m + 1)
                        act.copy(x_hi[:, 4 * g:4 * g + 4, t * P:(t + 1) * P],
                                 ps[:, 4 + 2 * t + g, :].rearrange("p (c s) -> p c s", c=4)).then_inc(x_split, 1)

            def split_high(count):
                for _ in range(count):
                    k = dense_splits[0]
                    name = SPLIT_HALVES[k]
                    at = HALF_AT[name]
                    act.wait_ge(dense_in[at % DENSE_SLOTS], 16 * (at // DENSE_SLOTS + 1))
                    if k >= HIGH_SLOTS:
                        wait_used(act, HALF_AT[SPLIT_HALVES[k - HIGH_SLOTS]])
                    act.copy(high_half(*name), raw_half(*name)).then_inc(dense_hi, 1)
                    dense_splits[0] += 1

            def take_piece(l, i):
                act.wait_ge(kv_psum, 2 * KV_P * l + i + 1)
                n = i // 2
                dst = k_mem[:, 0, n * N:(n + 1) * N] if n < 2 else v_mem[:, 0, (n - 2) * N:(n - 1) * N]
                act.copy(dst, ps[:, piece_bank(i), :]).then_inc(kv_act, 1)

            for n, (dst, src) in enumerate((
                (pos_i[:, :], a["positions"][0].rearrange("(t p) -> p t", p=P)),
                (rows[:, :], a["rows"]),
            )):
                act.dma_start(dst, src, allow_slow_non_contiguous=(n == 0)).then_inc(pos_in, 16)
            turn_split(TURN["x0"])
            def high(q, i, first=False):
                act.wait_ge(raw_in[q % RAW_SLOTS], 96 * i + 16 * (q // RAW_SLOTS + 1))
                if not first:
                    act.wait_ge(half_used, ITEM_HALVES * i + (q + 1))
                act.copy(w_hi[:, q % SPLIT_SLOTS, :], ring[:, q % RAW_SLOTS, :]).then_inc(hi_ready, 1)

            split_high(4)
            for dst, src in (
                (mask_a[:, :, :], a["mask_a"]), (mask_b[:, :, :], a["mask_b"]), (level[:, :, :], a["level"]),
                (lamv[:, :, 0, :], a["lam_q1"].unsqueeze(0).to_broadcast([P, DEPTH, AQ])),
                (lamv[:, :, 1, :], a["lam_k1"].unsqueeze(0).to_broadcast([P, DEPTH, AQ])),
                (lamv[:, :, 2, :], a["lam_q2"].unsqueeze(0).to_broadcast([P, DEPTH, AQ])),
                (lamv[:, :, 3, :], a["lam_k2"].unsqueeze(0).to_broadcast([P, DEPTH, AQ])),
                (g_a[:, :, :], a["diff_norm_g"].unsqueeze(0).to_broadcast([P, DEPTH, AV])),
                (g_c[:, :, :], a["gla_norm_g"].unsqueeze(0).to_broadcast([P, DEPTH, CV])),
                (ba[:, :, :], a["gla_ba"].unsqueeze(0).to_broadcast([P, DEPTH, CH * CK])),
                (wa2[:, :, :], a["gla_wa2"].rearrange("l r n -> r l n")),
                (w_router[:, :, :], a["moe_router"][0].rearrange("(c p) e -> p c e", p=P)),
            ):
                act.dma_start(dst, src).then_inc(const_in, 16)
            for l in range(DEPTH):
                act.dma_start(w_rank[:, l, :, :], a["w_in"][l].rearrange("(c p) n -> p c n", p=P)[:, :, C_RANK:])\
                    .then_inc(const_in, 16)
            act.wait_ge(angles, 1)
            act.activation(trig[:, :, :, :], angr[:, :, :, :], ACT.Sin).then_inc(trig_ready, 1)

            for l in range(DEPTH):
                for n in range(IN_P):
                    take(l, n, 0, h[:, 0, n * N:(n + 1) * N], h_act)
                    if l == 1 and n == 1:
                        turn_split(TURN["x3", l - 1], (1,))
                    if n == 1:
                        split_high(4)
                    if 2 <= n < IN_P - 2:
                        split_high(2)
                    if l == 0 and n == 1:
                        turn(TURN["mem"], memT)
                    if n == 2:
                        if l == 0:
                            act.wait_ge(const_in, 16 * CONSTS)
                        act.copy(wr_hi, w_rank[:, l, :, :]).then_inc(wr_high, 1)
                        act.wait_ge(lam_dots, l + 1)
                        act.activation(lams[:, 0:2], lams[:, 0:2], ACT.Exp).then_inc(lam_exps, 1)
                    if n == 4:
                        act.wait_ge(h_dve, IN_P * l + 5)
                        if l == 0:
                            act.wait_ge(pstep, 2)
                        else:
                            act.wait_ge(tr_psum[2], 2 * l)
                        act.mul(cpad[:, :, 0:CH, 0:CK], h[:, :, C_Q:C_K].rearrange("p t (h k) -> p t h k", h=CH),
                                CK ** -0.5).then_inc(cqk_ready, 1)
                        act.copy(cpad[:, :, CH:2 * CH, 0:CK],
                                 h[:, :, C_K:C_VAL].rearrange("p t (h k) -> p t h k", h=CH)).then_inc(cqk_ready, 1)
                act.wait_ge(rankT_psum, l + 1)
                act.copy(rankT, ps[0:CR, 0, 0:S]).then_inc(rankT_sb, 1)
                for r in (0, 2):
                    act.wait_ge(tr_psum[r], 2 * l + 1)
                    act.copy(tr[:, 2 * r:2 * r + 2, :], ps[:, 4 + r, :].rearrange("p (b s) -> p b s", b=2))\
                        .then_inc(tr_sb[r], 1)
                for r in (4, 6):
                    act.wait_ge(tr_psum[r % 4], 2 * l + 2)
                    act.copy(tr[:, 2 * r:2 * r + 2, :], ps[:, 4 + r % 4, :].rearrange("p (b s) -> p b s", b=2))\
                        .then_inc(tr_sb[r % 4], 1)

                def exps(u):
                    act.wait_ge(max_ready, UNITS * l + u + 1)
                    for i in range(4):
                        w = P * ((u if u < 4 else i) % 2 + 1)
                        ins = act.activation(s4[:, u % 2, i, 0:w], s4[:, u % 2, i, 0:w], ACT.Exp,
                                             bias=nmax[:, u % 2, i:i + 1], accum_out=sums[:, 4 * u + i:4 * u + i + 1])
                    ins.then_inc(probs_ready, 1)

                exps(0)
                act.wait_ge(z_abs, l + 1)
                done(act.activation(zz[:, 1, :], zz[:, 1, :], ACT.Exp, scale=-1.0))
                act.activation(zz[:, 1, :], zz[:, 1, :], ACT.Ln, bias=1.0).then_inc(z_ln, 1)
                take_piece(l, 0)
                for u in range(UNITS):
                    if u + 1 < UNITS:
                        exps(u + 1)
                    act.wait_ge(turn_ready, UNITS * l + u + 1)
                    c0, c1 = (0, 2) if u < 4 and u % 2 == 0 else (2, 6) if u < 4 else (0, 6)
                    if c0 == 0:
                        ins = act.copy(pT[:, 0:2, :], ps[:, 2, 0:2 * P].rearrange("p (c s) -> p c s", c=2))
                        if c1 > 2:
                            done(ins)
                    if c1 == 6:
                        ins = act.copy(pT[:, 2:6, :], ps[:, 3, :].rearrange("p (c s) -> p c s", c=4))
                    ins.then_inc(turn_taken, 1)
                    if u % 2:
                        take_piece(l, u + 1)
                    if u == 0:
                        act.wait_ge(decT_psum, l + 1)
                        act.copy(tr[:, 14:16, :], ps[:, 3, :].rearrange("p (b s) -> p b s", b=2)).then_inc(decT_sb, 1)
                    if u == 4:
                        act.wait_ge(dec_diff, l + 1)
                        done(act.activation(dec, dec, ACT.Abs))
                    if u == 5:
                        act.activation(dec, dec, ACT.Exp, scale=-1.0).then_inc(dec_exp, 1)
                act.activation(h[:, :, C_G:C_RANK], h[:, :, C_G:C_RANK], ACT.Silu).then_inc(gate_silu, 1)
                act.wait_ge(gla_out, l + 1)
                act.activation(zz[:, 0:2, :], ps[:, 2:4, 0:CH * CV], ACT.Square).then_inc(gla_square, 1)
                turn(TURN["k", l], kT)
                turn(TURN["mix", l], xT)
                act.wait_ge(tp_ready[3], TURN["mix", l] + 1)
                split_high(2)
                turn_split(TURN["x1", l], (0,))
                split_high(2)

                def cross_exps(t):
                    act.wait_ge(xmax_ready, T * l + t + 1)
                    for i in range(XH):
                        ins = act.activation(s4[:, t, i, :], cross_bank(t, i), ACT.Exp, bias=nmax[:, t, i:i + 1],
                                             scale=XD ** -0.5, accum_out=sums[:, 4 * t + i:4 * t + i + 1])
                    ins.then_inc(xp_ready, 1)

                def cross_turned(t):
                    act.wait_ge(xturn_ready, T * l + t + 1)
                    act.copy(pT_cross, ps[:, 4 + 2 * t:6 + 2 * t, :].rearrange("p b (c s) -> p (b c) s", c=4))\
                        .then_inc(xturn_taken, 1)

                for n in range(Q_P):
                    take(l, IN_P + KV_P + OUT_P + n, 0, q_tok[:, 0, n * N:(n + 1) * N], q_act)
                turn_split(TURN["x1", l], (1,))
                turn(TURN["q", l], xT, (0,))
                cross_exps(0)
                cross_turned(0)
                turn(TURN["q", l], xT, (1,))
                cross_exps(1)
                turn(TURN["xa", l], xT, (0,))
                cross_turned(1)
                turn(TURN["xa", l], xT, (1,))
                if l == 0:
                    split_high(2)
                    turn_split(TURN["x2", l], (0,))
                    split_high(2)
                else:
                    act.wait_ge(xo_ready, T * (l + 1))
                    for q in range(SPLIT_SLOTS):
                        high(q, 0, first=True)
                    turn(TURN["x2", l], xT)
                if l == 0:
                    for n in range(FFN_CHUNKS + 1):
                        if n < FFN_CHUNKS:
                            w = min(N, F_DENSE - n * N)
                            for t in range(T):
                                u = acc_use(l, MIX_PANELS + 2 * n)
                                act.wait_ge(acc_ready[t], u // 2 + 1)
                                if n >= 1:
                                    act.wait_ge(hg_ready, 2 * (n - 1) + t + 1)
                                act.activation(sg[:, t, 0:w], ps[:, t, 0:w], ACT.Silu).then_inc(silu_ready, 1)
                                act.wait_ge(silu_ready, 2 * n + t + 1)
                                act.sem_inc(acc_taken[t], 1)
                                if n == 0 and t == 0:
                                    turn_split(TURN["x2", l], (1,))
                            split_high(2)
                        if n >= 1:
                            m = n - 1
                            c = min(4, F_DENSE // P - 4 * m)
                            for t in range(T):
                                act.wait_ge(hT_psum[t], m + 1)
                                act.copy(h_hi[:, 4 * m:4 * m + c, t * P:(t + 1) * P],
                                         ps[:, 4 + 2 * (m % 2) + t, 0:c * P].rearrange("p (c s) -> p c s", c=c))\
                                    .then_inc(h_split, 1)
                        if n < FFN_CHUNKS:
                            split_high(2)
                    split_high(2 * W2_P - 1)
                    turn_split(TURN["x3", l], (0,))

            act.wait_ge(gate_diff, 1)
            act.activation(rmx[:, 2, :], rmx[:, 2, :], ACT.Exp).then_inc(gate_exp, 1)

            def misc(j, i, dst, groups, signal):
                q = 2 + j
                b, uses = q % 2, q // 2
                act.wait_ge(misc_ready[b], (uses + 1) if j < 0 else 7 * i + (uses + 1))
                act.copy(dst, ps[:, 6 + b, 0:groups * P].rearrange("p (c s) -> p c s", c=groups)).then_inc(signal, 1)

            def gather_high(i, j, g):
                misc(j + g, i, xe_hi[:, 4 * g:4 * g + 4, :], 4, xe_split)

            for g in range(2):
                gather_high(0, -2, g)
            act.sem_inc(g_taken, 1)
            act.sem_inc(y_act, 1)

            def take_y(i):
                act.wait_ge(half_used, ITEM_HALVES * i + (ITEM_HALVES + SPLIT_SLOTS))
                act.copy(y[:, 0:N], ps[:, 4, :]).then_inc(y_act, 1)

            def item(i, first=False):
                for q in range(SPLIT_SLOTS if first else 0, ITEM_HALVES):
                    high(q, i)
                    if q == SPLIT_SLOTS - 1:
                        take_y(i - 1)
                    if q % 4 == 0 and 4 <= q <= 4 * MOE_PAIRS:
                        n = q // 4 - 1
                        act.wait_ge(half_used, ITEM_HALVES * i + (4 * n + 2 + SPLIT_SLOTS))
                        if n >= 2:
                            act.wait_ge(he_ready, MOE_PAIRS * i + n)
                        act.activation(sge[:, n % 2, :], ps[:, 2 * (n % 2), :], ACT.Silu).then_inc(g_taken, 1)
                    if q in TURNED_AT:
                        n = TURNED_AT.index(q)
                        misc(n, i, he_hi[:, 4 * n:4 * n + 4, :], 4, he_split)
                    if q in GATHERED_AT:
                        gather_high(i, 7, GATHERED_AT.index(q))
                misc(9, i, gselT[:, :].rearrange("p (c s) -> p c s", c=2), 2, misc_taken[1])

            item(0, first=True)
            act.wait_ge(table_ready, 1)
            n_items = act.value_load(table_i[0:1, 0:1], min_val=NE, max_val=NE + EXTRA)
            last = act.value_load(table_i[0:1, 4:5], min_val=NE - 1, max_val=NE + EXTRA - 1)
            with act.Fori(1, n_items) as i:
                item(i)
            take_y(last)

        @block.vector
        def _(dve):
            step = [0]

            def done(ins):
                step[0] += 1
                ins.then_inc(vstep, 1)
                dve.wait_ge(vstep, step[0])

            signal_count = {h_dve.name: 0, q_dve.name: 0}

            def take(l, n, t, dst, signal):
                u = acc_use(l, n)
                b = 2 * (u % 2) + t
                dve.wait_ge(acc_ready[b], u // 2 + 1)
                dve.tensor_copy(dst, ps[:, b, :]).then_inc(signal, 1)
                signal_count[signal.name] += 1
                dve.wait_ge(signal, signal_count[signal.name])
                dve.sem_inc(acc_taken[b], 1)

            def turn(m, dst, tiles=range(T)):
                for t in tiles:
                    b = 2 * t + 1
                    dve.wait_ge(tp_ready[b], m + 1)
                    dve.tensor_copy(dst[:, 4:8, t * P:(t + 1) * P],
                                    ps[:, 4 + b, :].rearrange("p (c s) -> p c s", c=4)).then_inc(tp_taken[b], 1)

            def norm_of(k, n, width, meanwhile=None):
                done(dve.tensor_scalar(var[:, 0:n], var[:, 0:n], 1.0 / width, EPS, ALU.mult, ALU.add))
                dve.sem_inc(var_ready, 1)
                if meanwhile:
                    meanwhile()
                dve.wait_ge(rstd_ready, k + 1)

            def layer_norm(k, xx, t):
                xx = xx[:, t, :]
                done(dve.bn_aggr(mv[:, t, :], stats[:, t, :, :]))
                done(dve.tensor_scalar(var[:, t:t + 1], mv[:, t, 1:2], EPS, None, ALU.add))
                dve.sem_inc(var_ready, 1)
                dve.wait_ge(ln_in, 32 * (k + 1))
                done(dve.scalar_tensor_tensor(xx, xx, mv[:, t, 0:1], ln_gb[:, 0, :], ALU.subtract, ALU.mult))
                l, s = divmod(k, 3)
                dve.wait_ge(rstd_ready, POWERS * l + 3 + T * s + t)
                done(dve.scalar_tensor_tensor(xx, xx, rstd[:, t:t + 1], ln_gb[:, 1, :], ALU.mult, ALU.add))
                dve.sem_inc(ln_done, 1)

            def residual(l, n0, n, t):
                u = acc_use(l, n0 + n)
                b = 2 * (u % 2) + t
                dve.wait_ge(acc_ready[b], u // 2 + 1)
                xs = x[:, t, n * N:(n + 1) * N]
                done(dve.scalar_tensor_tensor(xs, xs, ALPHA, ps[:, b, :], ALU.mult, ALU.add))
                dve.sem_inc(acc_taken[b], 1)
                done(dve.bn_stats(stats[:, t, n, :], xs))

            x_turns, dense_splits = [0], [0]

            def turn_split(m, tiles=range(T)):
                for t in tiles:
                    for g in range(2):
                        x_turns[0] += 1
                        at = (slice(None), slice(4 * g, 4 * g + 4), slice(t * P, (t + 1) * P))
                        dve.wait_ge(x_split, x_turns[0])
                        dve.tensor_tensor(x_lo[at], ps[:, 4 + 2 * t + g, :].rearrange("p (c s) -> p c s", c=4),
                                          x_hi[at].bitcast(F32), ALU.subtract).then_inc(tp_taken[2 * t + g], 1)

            def split_low(count):
                for _ in range(count):
                    k = dense_splits[0]
                    name = SPLIT_HALVES[k]
                    dve.wait_ge(dense_hi, k + 1)
                    dve.tensor_tensor(low_half(*name), raw_half(*name), high_half(*name).bitcast(F32),
                                      ALU.subtract).then_inc(dense_lo, 1)
                    dense_splits[0] += 1

            def take_piece(l, i):
                dve.wait_ge(kv_psum, 2 * KV_P * l + i + 1)
                n = i // 2
                dst = k_mem[:, 1, n * N:(n + 1) * N] if n < 2 else v_mem[:, 1, (n - 2) * N:(n - 1) * N]
                dve.tensor_copy(dst, ps[:, piece_bank(i), :]).then_inc(kv_dve, 1)

            def low(q, i):
                dve.wait_ge(hi_ready, ITEM_HALVES * i + (q + 1))
                dve.tensor_tensor(w_lo[:, q % SPLIT_SLOTS, :], ring[:, q % RAW_SLOTS, :],
                                  w_hi[:, q % SPLIT_SLOTS, :].bitcast(F32), ALU.subtract).then_inc(lo_ready, 1)

            turn_split(TURN["x0"])
            split_low(4)
            dve.wait_ge(pos_in, 32)
            done(dve.tensor_copy(pos[:, :], pos_i[:, :]))
            done(dve.tensor_tensor(ang[:, 0, :, :], pos[:, :].unsqueeze(2).to_broadcast([P, T, ROPE]),
                                   freq.unsqueeze(1).to_broadcast([P, T, ROPE]), ALU.mult))
            done(dve.tensor_scalar(ang[:, 1, :, :], ang[:, 0, :, :], 1.0 / (2 * math.pi), MAGIC, ALU.mult, ALU.add))
            done(dve.tensor_scalar(ang[:, 1, :, :], ang[:, 1, :, :], MAGIC, None, ALU.subtract))
            af = ang[:, :, :, :].rearrange("p a t f -> p a (t f)")
            for c in PI2:
                done(dve.scalar_tensor_tensor(af[:, 0, :], af[:, 1, :], -c, af[:, 0, :], ALU.mult, ALU.add))
            done(dve.tensor_scalar(angr[:, 0, :, :], ang[:, 0, :, :], math.pi, -math.pi, ALU.min, ALU.max))
            rf = angr[:, :, :, :].rearrange("p a t f -> p a (t f)")
            done(dve.scalar_tensor_tensor(rf[:, 1, :], rf[:, 0, :], -1.0, rf[:, 0, :], ALU.mult, ALU.min))
            done(dve.tensor_scalar(angr[:, 1, :, :], angr[:, 1, :, :], math.pi / 2, None, ALU.add))
            dve.sem_inc(angles, 1)

            def rope(base, heads, width, pairs, stride):
                v = h[:, :, base:base + heads * width].rearrange("p t (h k) -> p t h k", k=width)
                x1, x2 = v[:, :, :, 0:pairs], v[:, :, :, pairs:2 * pairs]
                shape = [P, T, heads, pairs]
                sn, cs = (trig[:, n, :, ::stride].unsqueeze(2).to_broadcast(shape) for n in range(2))
                w = [rt[:, n, :, 0:heads * pairs].rearrange("p t (h k) -> p t h k", k=pairs) for n in range(4)]
                for o, p, q in ((0, x1, cs), (1, x2, sn), (2, x2, cs), (3, x1, sn)):
                    for t in range(T):
                        ins = dve.tensor_tensor(w[o][:, t], p[:, t], q[:, t], ALU.mult)
                done(ins)
                for t in range(T):
                    dve.tensor_tensor(x1[:, t], w[0][:, t], w[1][:, t], ALU.subtract)
                    ins = dve.tensor_tensor(x2[:, t], w[2][:, t], w[3][:, t], ALU.add)
                done(ins)

            for l in range(DEPTH):
                lam_init = 0.8 - 0.6 * math.exp(-0.3 * l)
                for n in range(IN_P):
                    if l == 1 and n == 0:
                        layer_norm(2, x, 1)
                        turn_split(TURN["x3", l - 1], (1,))
                    take(l, n, 1, h[:, 1, n * N:(n + 1) * N], h_dve)
                    if n < IN_P - 2:
                        split_low(2)
                    if l == 0 and n == 1:
                        turn(TURN["mem"], memT)
                        dve.wait_ge(const_in, 16 * CONSTS)
                    if n == 1:
                        lv = lamv[:, l, :, :].rearrange("p (m two) k -> p m two k", two=2)
                        done(dve.tensor_tensor(lamp[:, :, :], lv[:, :, 0, :], lv[:, :, 1, :], ALU.mult))
                        done(dve.tensor_reduce(lams[:, 0:2], lamp[:, :, :], AX, ALU.add))
                        dve.sem_inc(lam_dots, 1)
                        done(dve.tensor_scalar(g_a[:, l, :], g_a[:, l, :], 1.0 - lam_init, None, ALU.mult))
                    if n == 2:
                        dve.wait_ge(h_act, IN_P * l + 3)
                        dve.wait_ge(trig_ready, 1)
                        rope(A_Q, 2 * 2 * AH, AQ, AQ // 8, 2)
                        rope(B_Q, 2 * BH, BD, BD // 8, 1)
                        dve.sem_inc(rope_done, 1)
                    if n == 4:
                        dve.wait_ge(wr_high, l + 1)
                        dve.tensor_tensor(wr_lo, w_rank[:, l, :, :], wr_hi.bitcast(F32), ALU.subtract).then_inc(wr_ready, 1)
                        dve.wait_ge(lam_exps, l + 1)
                        done(dve.tensor_tensor(lams[:, 2:3], lams[:, 1:2], lams[:, 0:1], ALU.subtract))
                        done(dve.tensor_scalar(lams[:, 3:4], lams[:, 2:3], -lam_init, None, ALU.add))
                for r in (1, 3, 5):
                    b = r % 4
                    dve.wait_ge(tr_psum[b], (l if b == 3 else 2 * l + r // 4) + 1)
                    dve.tensor_copy(tr[:, 2 * r:2 * r + 2, :], ps[:, 4 + b, :].rearrange("p (b s) -> p b s", b=2))\
                        .then_inc(tr_sb[b], 1)

                def masked_max(u):
                    U = UNITS * l + u
                    dve.wait_ge(scores_ready, U + 1)
                    if u >= 2:
                        dve.wait_ge(turn_ready, U - 1)
                    for i in range(4):
                        t = u % 2 if u < 4 else i % 2
                        w = P * (t + 1)
                        m, sc = (mask_a, AQ ** -0.5) if u < 4 else (mask_b, BD ** -0.5)
                        ins = dve.scalar_tensor_tensor(s4[:, u % 2, i, 0:w], score_view(u, i), sc, m[:, t, 0:w],
                                                       ALU.mult, ALU.add)
                        if i < 3:
                            ins.then_inc(score_taken, 1)
                    done(ins)
                    dve.sem_inc(score_taken, 1)
                    if u < 4:
                        w = P * (u % 2 + 1)
                        done(dve.tensor_reduce(nmax[:, u % 2, :], s4[:, u % 2, :, 0:w], AX, ALU.max, negate=True))
                    else:
                        for t in range(T):
                            ins = dve.tensor_reduce(nmax[:, u % 2, t::2], s4[:, u % 2, t::2, 0:P * (t + 1)], AX, ALU.max,
                                                    negate=True)
                        done(ins)
                    dve.sem_inc(max_ready, 1)

                def difference(u):
                    dve.wait_ge(probs_ready, UNITS * l + u + 1)
                    rs = rsum[:, 4 * u:4 * u + 4]
                    done(dve.reciprocal(rs, sums[:, 4 * u:4 * u + 4]))
                    done(dve.tensor_scalar(rs[:, 1::2], rs[:, 1::2], lams[:, 3:4], None, ALU.mult))
                    w = P * (u % 2 + 1)
                    for j in range(2):
                        ins = dve.tensor_scalar(s4[:, u % 2, 2 * j + 1, 0:w], s4[:, u % 2, 2 * j + 1, 0:w],
                                                rs[:, 2 * j + 1:2 * j + 2], None, ALU.mult)
                    done(ins)
                    for j in range(2):
                        ins = dve.scalar_tensor_tensor(s4[:, u % 2, 2 * j, 0:w], s4[:, u % 2, 2 * j, 0:w],
                                                       rs[:, 2 * j:2 * j + 1], s4[:, u % 2, 2 * j + 1, 0:w],
                                                       ALU.mult, ALU.add)
                    ins.then_inc(diff_ready, 1)

                bc = qk[:, 1, 0, :].rearrange("p (a t s) -> p a t s", a=2, t=T)

                def level_exponents(v):
                    half = (P // 2) >> v
                    bv = qk[:, 1, 0, :].rearrange("p (n w) -> p n w", w=2 * half)
                    dve.tensor_tensor(dec[:, v, :].rearrange("p (n w) -> p n w", w=2 * half), bv,
                                      bv[:, :, half - 1:half].to_broadcast([P, 2 * S // (2 * half), 2 * half]),
                                      ALU.subtract)

                masked_max(0)
                dve.wait_ge(z_psum, l + 1)
                z3 = zz.rearrange("p a (t n) -> p a t n", t=T)
                done(dve.tensor_tensor(z3[:, 0], ps[:, 2, 0:T * CH * CK].rearrange("p (t n) -> p t n", t=T),
                                       ba[:, l, :].unsqueeze(1).to_broadcast([P, T, CH * CK]), ALU.add))
                done(dve.scalar_tensor_tensor(zz[:, 1, :], zz[:, 0, :], -1.0, zz[:, 0, :], ALU.mult, ALU.max))
                dve.sem_inc(z_abs, 1)
                oa = o_tok[:, :, 0:S].rearrange("p t (h k) -> p t h k", h=AH)
                for u in range(UNITS):
                    if u + 1 < UNITS:
                        masked_max(u + 1)
                    if u < 4:
                        difference(u)
                    if u % 2 == 0:
                        take_piece(l, u + 1)
                    if u == 0:
                        done(dve.tensor_scalar(zz[:, 0, :], zz[:, 0, :], 0.0, 1.0 / TAU, ALU.min, ALU.mult))
                        dve.wait_ge(z_ln, l + 1)
                        done(dve.tensor_scalar(zz[:, 2, :], zz[:, 1, :], -1.0 / TAU, None, ALU.mult))
                        if l == 0:
                            dve.wait_ge(pstep, 2)
                        zh = zz.rearrange("p a (t h k) -> p a t h k", t=T, h=CH)
                        for t in range(T):
                            ins = dve.tensor_tensor(cpad[:, t, 2 * CH:3 * CH, 0:CK], zh[:, 0, t], zh[:, 2, t], ALU.add)
                        ins.then_inc(decay_ready, 1)
                    if u == 1:
                        dve.wait_ge(decT_sb, l + 1)
                        for pair in range(2):
                            for t in range(T):
                                ins = dve.tensor_tensor_scan(bc[:, pair, t, :], ones, tr[:, 14 + pair, t * P:(t + 1) * P],
                                                             0.0, ALU.mult, ALU.add)
                        done(ins)
                    if 1 <= u < 4:
                        for v in (range(0, 2), range(2, 4), range(4, LEVELS))[u - 1]:
                            level_exponents(v)
                    if u == 3:
                        d7 = dec[:, 7, :].rearrange("p (a t s) -> p a t s", a=2, t=T)
                        dve.tensor_tensor(d7[:, :, 0, :], bc[:, :, 0, :], bc[:, :, 0, P - 1:P].to_broadcast([P, 2, P]),
                                          ALU.subtract)
                        done(dve.tensor_copy(d7[:, :, 1, :], bc[:, :, 1, :]))
                        dve.sem_inc(dec_diff, 1)
                    if u == 4:
                        dve.wait_ge(pv_done, UNITS * l + 4)
                        done(dve.tensor_copy(o_tok[:, :, 0:S], ps[:, 0, :].rearrange("p (t n) -> p t n", t=T)))
                        dve.sem_inc(oa_taken, 1)
                    if u == 5:
                        done(dve.tensor_tensor(oa_sq, o_tok[:, :, 0:S], o_tok[:, :, 0:S], ALU.mult))
                        done(dve.tensor_reduce(var[:, :].rearrange("p (t h) -> p t h", t=T),
                                               oa_sq.rearrange("p t (h k) -> p t h k", h=AH), AX, ALU.add))
                        norm_of(POWERS * l, 8, AV)
                    if u == 6:
                        rb = rstd[:, :].rearrange("p (t h) -> p t h", t=T).unsqueeze(3).to_broadcast([P, T, AH, AV])
                        done(dve.tensor_tensor(oa, oa, rb, ALU.mult))
                        gb = g_a[:, l, :].unsqueeze(1).to_broadcast([P, AH, AV])
                        for t in range(T):
                            dve.tensor_tensor(oa[:, t], oa[:, t], gb, ALU.mult)

                def dilated_output():
                    done(dve.reciprocal(rsum[:, 16:28], sums[:, 16:28]))
                    for t in range(T):
                        rv = rsum[:, 16 + t:28:2].unsqueeze(2).to_broadcast([P, BH, BD])
                        done(dve.tensor_tensor(o_tok[:, t, S:S + BH * BD].rearrange("p (h k) -> p h k", h=BH),
                                               ps[:, 1 - t, 0:BH * BD].rearrange("p (h k) -> p h k", h=BH), rv, ALU.mult))

                dve.wait_ge(dec_exp, l + 1)

                def products(s):
                    if s >= 3:
                        dve.wait_ge(level_scores, GSTEPS * l + s - 1)
                    for n in range(2):
                        ins = dve.tensor_tensor(qk[:, s % 2, n, :], tr[:, 10 + 2 * n:12 + 2 * n, :].rearrange("p b s -> p (b s)"),
                                                dec[:, s - 1, :], ALU.mult)
                    ins.then_inc(level_ready, 1)

                def combine(s):
                    dve.wait_ge(level_scores, GSTEPS * l + s + 1)
                    for hp in range(2):
                        src = ps[:, 4 + 2 * hp + s % 2, :].rearrange("p (b q) -> p b q", b=4)
                        if s == 0:
                            ins = dve.tensor_tensor(st[:, hp], src, ident.unsqueeze(1).to_broadcast([P, 4, P]), ALU.mult)
                        elif s <= LEVELS:
                            ins = dve.copy_predicated(st[:, hp], level[:, s - 1, :].unsqueeze(1).to_broadcast([P, 4, P]), src)
                        else:
                            ins = dve.tensor_copy(stx[:, hp], src[:, 0:2, :])
                    done(ins)
                    dve.sem_inc(level_taken, 1)

                products(1)
                dve.wait_ge(pv_done, UNITS * (l + 1))
                for s in range(GSTEPS):
                    if s + 2 < GSTEPS:
                        products(s + 2)
                    combine(s)
                    if s == 1:
                        dilated_output()
                dve.wait_ge(gla_square, l + 1)
                done(dve.tensor_reduce(var[:, :].rearrange("p (t h) -> p t h", t=T),
                                       zz[:, 0:2, :].rearrange("p t (h k) -> p t h k", h=CH), AX, ALU.add))
                norm_of(POWERS * l + 1, 8, CV, lambda: turn(TURN["k", l], kT))
                dve.wait_ge(gate_silu, l + 1)
                for t in range(T):
                    oc = o_tok[:, t, S + BH * BD:D].rearrange("p (h k) -> p h k", h=CH)
                    done(dve.tensor_tensor(oc, ps[:, 2 + t, 0:CH * CV].rearrange("p (h k) -> p h k", h=CH),
                                           rstd[:, 4 * t:4 * t + 4].unsqueeze(2).to_broadcast([P, CH, CV]), ALU.mult))
                    done(dve.tensor_tensor(oc, oc, g_c[:, l, :].unsqueeze(1).to_broadcast([P, CH, CV]), ALU.mult))
                    oc = o_tok[:, t, S + BH * BD:D]
                    done(dve.tensor_tensor(oc, oc, h[:, t, C_G:C_RANK], ALU.mult))
                    dve.sem_inc(mixed, 1)
                turn(TURN["mix", l], xT)
                out_p = IN_P + KV_P
                residual(l, out_p, 0, 0)
                residual(l, out_p, 1, 0)
                layer_norm(3 * l, x, 0)
                split_low(1)
                residual(l, out_p, 0, 1)
                split_low(1)
                residual(l, out_p, 1, 1)
                turn_split(TURN["x1", l], (0,))
                split_low(2)
                layer_norm(3 * l, x, 1)
                turn_split(TURN["x1", l], (1,))

                def take_q(n):
                    take(l, IN_P + KV_P + OUT_P + n, 1, q_tok[:, 1, n * N:(n + 1) * N], q_dve)

                def cross_max(t):
                    dve.wait_ge(xs_ready, T * l + t + 1)
                    banks = ps[:, 4 + 2 * t:6 + 2 * t, :].rearrange("p b (i s) -> p (b i) s", i=2)
                    done(dve.tensor_reduce(nmax[:, t, :], banks, AX, ALU.max, negate=True))
                    done(dve.tensor_scalar(nmax[:, t, :], nmax[:, t, :], XD ** -0.5, None, ALU.mult))
                    dve.sem_inc(xmax_ready, 1)

                def cross_output(t):
                    dve.wait_ge(xp_ready, T * l + t + 1)
                    done(dve.reciprocal(rsum[:, 4 * t:4 * t + 4], sums[:, 4 * t:4 * t + 4]))
                    dve.wait_ge(xo_ready, T * l + t + 1)
                    for g in range(2):
                        ins = dve.tensor_tensor(
                            o_xa[:, t, g * N:(g + 1) * N].rearrange("p (h k) -> p h k", h=2),
                            ps[:, t + 2 * g, :].rearrange("p (h k) -> p h k", h=2),
                            rsum[:, 4 * t + 2 * g:4 * t + 2 * g + 2].unsqueeze(2).to_broadcast([P, 2, XD]), ALU.mult)
                    done(ins)
                    dve.sem_inc(xo_taken, 1)

                o_p = IN_P + KV_P + OUT_P + Q_P
                turn(TURN["q", l], xT, (0,))
                take_q(0)
                cross_max(0)
                take_q(1)
                turn(TURN["q", l], xT, (1,))
                cross_output(0)
                cross_max(1)
                turn(TURN["xa", l], xT, (0,))
                residual(l, o_p, 0, 0)
                cross_output(1)
                residual(l, o_p, 1, 0)
                turn(TURN["xa", l], xT, (1,))
                layer_norm(3 * l + 1, x, 0)
                if l == 0:
                    split_low(1)
                else:
                    low(0, 0)
                residual(l, o_p, 0, 1)
                if l == 0:
                    split_low(1)
                residual(l, o_p, 1, 1)
                if l == 0:
                    turn_split(TURN["x2", l], (0,))
                    split_low(2)
                    layer_norm(3 * l + 1, x, 1)
                    turn_split(TURN["x2", l], (1,))
                else:
                    turn(TURN["x2", l], xT, (0,))
                    layer_norm(3 * l + 1, x, 1)
                    turn(TURN["x2", l], xT, (1,))
                if l == 0:
                    for n in range(FFN_CHUNKS + 1):
                        if n < FFN_CHUNKS:
                            w = min(N, F_DENSE - n * N)
                            if n:
                                split_low(2)
                            for t in range(T):
                                u = acc_use(l, MIX_PANELS + 2 * n + 1)
                                dve.wait_ge(silu_ready, 2 * n + t + 1)
                                dve.wait_ge(acc_ready[2 + t], u // 2 + 1)
                                if n >= 2:
                                    dve.wait_ge(hT_psum[t], n - 1)
                                dve.tensor_tensor(hg[:, n % 2, t, 0:w], sg[:, t, 0:w], ps[:, 2 + t, 0:w], ALU.mult)\
                                    .then_inc(hg_ready, 1)
                                dve.wait_ge(hg_ready, 2 * n + t + 1)
                                dve.sem_inc(acc_taken[2 + t], 1)
                                if n == 0 and t == 0:
                                    split_low(2)
                        if n >= 1:
                            m = n - 1
                            c = min(4, F_DENSE // P - 4 * m)
                            for t in range(T):
                                at = (slice(None), slice(4 * m, 4 * m + c), slice(t * P, (t + 1) * P))
                                dve.wait_ge(h_split, 2 * m + t + 1)
                                dve.tensor_tensor(h_lo[at],
                                                  ps[:, 4 + 2 * (m % 2) + t, 0:c * P].rearrange("p (c s) -> p c s", c=c),
                                                  h_hi[at].bitcast(F32), ALU.subtract).then_inc(hT_sb[t], 1)
                        if n < FFN_CHUNKS:
                            split_low(2)
                    split_low(2 * W2_P - 1 - 4)
                    for t in range(T):
                        dve.wait_ge(w2_ready, t + 1)
                        for n in range(2):
                            xs = x[:, t, n * N:(n + 1) * N]
                            done(dve.scalar_tensor_tensor(xs, xs, ALPHA, ps[:, t + 2 * n, :], ALU.mult, ALU.add))
                            done(dve.bn_stats(stats[:, t, n, :], xs))
                        if t == 0:
                            layer_norm(3 * l + 2, x, 0)
                            split_low(1)
                    turn_split(TURN["x3", l], (0,))
                    split_low(3)

            low(1, 0)
            low(2, 0)
            dve.wait_ge(logit_psum, 1)
            dve.tensor_scalar(acc, x[:, :, :], ALPHA, None, ALU.mult).then_inc(acc_init, 1)
            full = [P, T, NE]

            def over(v):
                return v.unsqueeze(2).to_broadcast(full)

            done(dve.tensor_copy(lg[:, 0], ps[:, 4, 0:T * NE].rearrange("p (t e) -> p t e", t=T)))
            for c in range(2):
                done(dve.tensor_reduce(rmx[:, c, :], lg[:, c], AX, ALU.max))
                done(dve.tensor_tensor(rtmp[:, :, :], lg[:, c], over(rmx[:, c, :]), ALU.is_equal))
                done(dve.tensor_tensor(rtmp[:, :, :], rtmp[:, :, :], desc.unsqueeze(1).to_broadcast(full), ALU.mult))
                done(dve.tensor_reduce(rmx[:, 3, :], rtmp[:, :, :], AX, ALU.max))
                done(dve.tensor_tensor(oh[:, c], rtmp[:, :, :], over(rmx[:, 3, :]), ALU.is_equal))
                if c == 0:
                    done(dve.tensor_scalar(rtmp[:, :, :], oh[:, 0], -3e38, None, ALU.mult))
                    done(dve.tensor_tensor(lg[:, 1], rtmp[:, :, :], lg[:, 0], ALU.add))
            done(dve.tensor_tensor(chosen[:, :, :], oh[:, 0], oh[:, 1], ALU.add))
            dve.sem_inc(chosen_ready, 1)
            done(dve.memset(slot[:, :, :], -1.0))
            dve.wait_ge(rank2_psum, 1)
            done(dve.tensor_tensor(rtmp[:, :, :], ps[:, 5, 0:T * NE].rearrange("p (t e) -> p t e", t=T), chosen[:, :, :],
                                   ALU.mult))
            done(dve.tensor_scalar(lg[:, 0], chosen[:, :, :], -1.0, 1000.0, ALU.add, ALU.mult))
            done(dve.tensor_tensor(slot[:, :, 0:NE], rtmp[:, :, :], lg[:, 0], ALU.add))
            def select(i):
                for t in range(T):
                    ins = dve.tensor_scalar(sel[:, t, :], iota, slot[:, t, bass.ds(i, 1)], None, ALU.is_equal)
                ins.then_inc(sel_ready, 1)

            done(dve.tensor_tensor(rmx[:, 2, :], rmx[:, 1, :], rmx[:, 0, :], ALU.subtract))
            dve.sem_inc(gate_diff, 1)
            select(0)
            dve.sem_inc(he_ready, 1)
            dve.sem_inc(y_dve, 1)

            def misc_low(j, i, hi, lo, split, count):
                b = j % 2
                dve.wait_ge(split, count)
                dve.tensor_tensor(lo, ps[:, 6 + b, :].rearrange("p (c s) -> p c s", c=4), hi.bitcast(F32),
                                  ALU.subtract).then_inc(misc_taken[b], 1)

            def gather_low(i, j, g, count):
                misc_low(j + g, i, xe_hi[:, 4 * g:4 * g + 4, :], xe_lo[:, 4 * g:4 * g + 4, :], xe_split, count)

            for g in range(2):
                gather_low(0, -2, g, g + 1)
            dve.wait_ge(gate_exp, 1)
            done(dve.tensor_scalar(rmx[:, 3, :], rmx[:, 2, :], 1.0, None, ALU.add))
            done(dve.reciprocal(rmx[:, 0, :], rmx[:, 3, :]))
            done(dve.tensor_tensor(rmx[:, 1, :], rmx[:, 0, :], rmx[:, 2, :], ALU.mult))
            done(dve.memset(gates[:, :, :], 0.0))
            done(dve.tensor_tensor(gates[:, :, 0:NE], oh[:, 0], over(rmx[:, 0, :]), ALU.mult))
            done(dve.tensor_tensor(rtmp[:, :, :], oh[:, 1], over(rmx[:, 1, :]), ALU.mult))
            done(dve.tensor_tensor(gates[:, :, 0:NE], gates[:, :, 0:NE], rtmp[:, :, :], ALU.add))

            def extra_items(part):
                if part == 0:
                    done(dve.tensor_scalar(cnt[:, 0, :], ps[:, 5, 32:32 + NE], float(P), None, ALU.is_gt))
                    done(dve.tensor_tensor_scan(cnt[:, 1, :], ones[:, 0:NE], cnt[:, 0, :], 0.0, ALU.mult, ALU.add))
                    done(dve.tensor_scalar(table[:, 0:1], cnt[:, 1, NE - 1:NE], float(NE), None, ALU.add))
                    done(dve.tensor_tensor(cnt[:, 2, :], cnt[:, 1, :], cnt[:, 0, :], ALU.subtract))
                elif part <= EXTRA:
                    r = part - 1
                    done(dve.tensor_scalar(wr[:, r, :], cnt[:, 2, :], float(r), None, ALU.is_equal))
                    done(dve.tensor_tensor(wr[:, r, :], wr[:, r, :], cnt[:, 0, :], ALU.mult))
                    wb = wr[:, r, :].unsqueeze(1).to_broadcast(full)
                    done(dve.tensor_tensor(cnt[:, 3, :], wr[:, r, :], eid, ALU.mult))
                    done(dve.tensor_reduce(table[:, r + 1:r + 2], cnt[:, 3, :], AX, ALU.add))
                    done(dve.tensor_tensor(rtmp[:, :, :], gates[:, :, 0:NE], wb, ALU.mult))
                    done(dve.tensor_reduce(gates[:, :, NE + r:NE + r + 1].rearrange("p t o -> p (t o)"), rtmp[:, :, :], AX, ALU.add))
                    done(dve.tensor_scalar(rtmp[:, :, :], slot[:, :, 0:NE], float(P), None, ALU.subtract))
                    done(dve.tensor_tensor(rtmp[:, :, :], rtmp[:, :, :], wb, ALU.mult))
                    done(dve.tensor_reduce(slot[:, :, NE + r:NE + r + 1].rearrange("p t o -> p (t o)"), rtmp[:, :, :], AX, ALU.add))
                else:
                    done(dve.tensor_scalar(table[:, 4:5], table[:, 0:1], -1.0, None, ALU.add))
                    done(dve.tensor_copy(table_i[:, :], table[:, :]))
                    dve.sem_inc(table_ready, 1)

            def take_y(i):
                dve.wait_ge(half_used, ITEM_HALVES * i + (ITEM_HALVES + SPLIT_SLOTS))
                dve.tensor_copy(y[:, N:D], ps[:, 5, :]).then_inc(y_dve, 1)

            def add_up(i, j):
                t, n = divmod(j - 10, 2)
                b, uses = j % 2, (2 + j) // 2
                dve.wait_ge(misc_ready[b], 7 * i + (uses + 1))
                xs = acc[:, t, n * N:(n + 1) * N]
                dve.tensor_tensor(xs, xs, ps[:, 6 + b, :], ALU.add).then_inc(misc_taken[b], 1)

            def item(i, first=False):
                for t in range(T):
                    ins = dve.tensor_scalar(gsel[:, t, :], iota, slot[:, t, bass.ds(i, 1)], gates[:, t, bass.ds(i, 1)],
                                            ALU.is_equal, ALU.mult)
                ins.then_inc(gsel_ready, 1)
                for q in range(SPLIT_SLOTS if first else 0, ITEM_HALVES):
                    low(q, i)
                    if first and q in EXTRAS_AT:
                        extra_items(EXTRAS_AT.index(q))
                    if not first and q == SPLIT_SLOTS - 1:
                        take_y(i - 1)
                    if not first and q in ADDED_AT:
                        add_up(i - 1, 10 + ADDED_AT.index(q))
                    if q % 4 == 2 and 6 <= q <= 4 * MOE_PAIRS + 2:
                        n = (q - 6) // 4
                        dve.wait_ge(g_taken, MOE_PAIRS * i + (n + 2))
                        dve.wait_ge(half_used, ITEM_HALVES * i + (4 * n + 4 + SPLIT_SLOTS))
                        if n >= 2:
                            dve.wait_ge(misc_ready[n % 2], 7 * i + (n // 2 + 1))
                        dve.tensor_tensor(hge[:, n % 2, :], sge[:, n % 2, :], ps[:, 2 * (n % 2) + 1, :], ALU.mult)\
                            .then_inc(he_ready, 1)
                    if q == 20:
                        select(i + 1)
                    if q in TURNED_AT:
                        n = TURNED_AT.index(q)
                        misc_low(n, i, he_hi[:, 4 * n:4 * n + 4, :], he_lo[:, 4 * n:4 * n + 4, :], he_split,
                                 MOE_PAIRS * i + (n + 1))
                    if q in GATHERED_AT:
                        g = GATHERED_AT.index(q)
                        gather_low(i, 7, g, 2 * i + (g + 3))

            item(0, first=True)
            n_items = dve.value_load(table_i[0:1, 0:1], min_val=NE, max_val=NE + EXTRA)
            last = dve.value_load(table_i[0:1, 4:5], min_val=NE - 1, max_val=NE + EXTRA - 1)
            with dve.Fori(1, n_items) as i:
                item(i)
            take_y(last)
            for j in range(10, 14):
                add_up(last, j)
            for b in range(2):
                dve.wait_ge(misc_taken[b], 7 * last + 8)
            for t in range(T):
                for g in range(2):
                    done(dve.bn_stats(stats[:, t, g, :], acc[:, t, g * N:(g + 1) * N]))
                layer_norm(5, acc, t)

        @block.tensor
        def _(pe):
            def turn_tile(m, src, t):
                for g in range(2):
                    b = 2 * t + g
                    if m:
                        pe.wait_ge(tp_taken[b], m)
                    for c in range(4):
                        k = 4 * g + c
                        ins = pe.transpose(ps[:, 4 + b, c * P:(c + 1) * P], src[:, t, k * P:(k + 1) * P], ident)
                    ins.then_inc(tp_ready[b], 1)

            def turned(m, t):
                for b in (2 * t, 2 * t + 1):
                    pe.wait_ge(tp_taken[b], m + 1)

            HI_LO = ((0, 0), (0, 1), (1, 0))

            def half_ready(l, n, g):
                if (l, n, g) in SPLIT_AT:
                    pe.wait_ge(dense_lo, SPLIT_AT[l, n, g] + 1)
                else:
                    at = HALF_AT[l, n, g]
                    pe.wait_ge(dense_in[at % DENSE_SLOTS], 16 * (at // DENSE_SLOTS + 1))

            def gemm(l, n, tiles=range(T), chunks=range(KC)):
                u = acc_use(l, n)
                _, _, w = w_panel(l, n).shape
                split = (l, n, 0) in SPLIT_AT
                for t in tiles:
                    b = 2 * (u % 2) + t
                    if u >= 2 and chunks[0] == 0:
                        pe.wait_ge(acc_taken[b], u // 2)
                    for g in range(2):
                        if 4 * g not in chunks:
                            continue
                        if t == 0:
                            half_ready(l, n, g)
                        if split:
                            weights = (high_half(l, n, g), low_half(l, n, g))
                            passes = [((x_hi, x_lo)[p], weights[q]) for p, q in HI_LO]
                        else:
                            passes = [(xT, raw_half(l, n, g))]
                        for m, (lhs, rhs) in enumerate(passes):
                            for c in range(4):
                                ins = pe.matmul(ps[:, b, 0:w], lhs[:, 4 * g + c, t * P:(t + 1) * P], rhs[:, c, :],
                                                start=(g == 0 and m == 0 and c == 0),
                                                stop=(g == 1 and m == len(passes) - 1 and c == 3))
                        if t == T - 1 and g == 0:
                            ins.then_inc(dense_used, 1)
                    if chunks[-1] == KC - 1:
                        ins.then_inc(acc_ready[b], 1)

            def gemm_pair(l, n, t):
                gemm(l, n, (t,))
                gemm(l, n + 1, (t,))

            def piece(l, i, chunks=range(KC)):
                n, t = divmod(i, 2)
                if chunks[0] == 0:
                    if i == 0:
                        pe.wait_ge(acc_taken[1], acc_use(l, 4) // 2 + 1)
                    elif i <= 4 or i == 7:
                        before_ = i - 1 if i <= 4 else 5
                        pe.wait_ge((kv_act, kv_dve)[before_ % 2], KV_P * l + before_ // 2 + 1)
                for k in chunks:
                    g, c = divmod(k, 4)
                    if c == 0 and t == 0:
                        half_ready(l, IN_P + n, g)
                    ins = pe.matmul(ps[:, piece_bank(i), :], memT[:, k, t * P:(t + 1) * P],
                                    raw_half(l, IN_P + n, g)[:, c, :], start=(k == 0), stop=(k == KC - 1))
                    if k == 3 and t == 1:
                        ins.then_inc(dense_used, 1)
                if chunks[-1] == KC - 1:
                    ins.then_inc(kv_psum, 1)

            pe.wait_ge(x_in, 32)
            for t in range(T):
                turn_tile(TURN["x0"], x, t)
            for t in range(T):
                turned(TURN["x0"], t)

            for l in range(DEPTH):
                if l == 0:
                    gemm_pair(l, 0, 0)
                else:
                    turned(TURN["x3", l - 1], 0)
                    gemm_pair(l, 0, 0)
                    pe.wait_ge(ln_done, T * 3 * l)
                    turn_tile(TURN["x3", l - 1], x, 1)
                    turned(TURN["x3", l - 1], 1)
                gemm_pair(l, 0, 1)
                if l == 0:
                    pe.wait_ge(mem_in, 16)
                    for t in range(T):
                        turn_tile(TURN["mem"], mem_tok, t)
                for n in range(2, IN_P):
                    gemm(l, n)
                if l == 0:
                    for t in range(T):
                        turned(TURN["mem"], t)
                    pe.wait_ge(const_in, 16 * CONSTS)
                pe.wait_ge(acc_taken[0], acc_use(l, 4) // 2 + 1)
                pe.wait_ge(wr_ready, l + 1)
                for m, (p, q) in enumerate(HI_LO):
                    for k in range(KC):
                        ins = pe.matmul(ps[0:CR, 0, 0:S], (wr_hi, wr_lo)[q][:, k, :], (x_hi, x_lo)[p][:, k, :],
                                        start=(m == 0 and k == 0), stop=(m == 2 and k == KC - 1))
                ins.then_inc(rankT_psum, 1)

                def turn_heads(r, bank):
                    for c in range(2):
                        blk = 2 * r + c
                        for t in range(T):
                            if blk < 4:
                                src = h[:, t, blk * P:(blk + 1) * P]
                            elif blk < 10:
                                src = h[:, t, B_Q + (blk - 4) * P:B_Q + (blk - 3) * P]
                            else:
                                src = cpad[:, t, 2 * (blk - 10):2 * (blk - 9), :].rearrange("p h k -> p (h k)")
                            ins = pe.transpose(ps[:, bank, (2 * c + t) * P:(2 * c + t + 1) * P], src, ident)
                    return ins

                pe.wait_ge(rope_done, l + 1)
                for r in range(7):
                    b = r % 4
                    if r == 5:
                        pe.wait_ge(cqk_ready, 2 * (l + 1))
                    if r >= 4:
                        pe.wait_ge(tr_sb[b], 2 * l + 1)
                    turn_heads(r, 4 + b).then_inc(tr_psum[b], 1)
                pe.wait_ge(acc_taken[2], acc_use(l, 5) // 2 + 1)
                pe.wait_ge(rankT_sb, l + 1)
                for t in range(T):
                    ins = pe.matmul(ps[:, 2, t * CH * CK:(t + 1) * CH * CK], rankT[:, t * P:(t + 1) * P], wa2[:, l, :],
                                    start=True, stop=True)
                ins.then_inc(z_psum, 1)
                for b in range(4):
                    pe.wait_ge(tr_sb[b], (2 if b < 3 else 1) * (l + 1))

                def scores(u):
                    pe.wait_ge(score_taken, 4 * (UNITS * l + u)) if u or l else None
                    for i in range(4):
                        if u < 4:
                            t, blk, r0, rn = u % 2, u // 2, AQ * i, AQ
                            q, k = tr[:, blk, :], tr[:, 2 + blk, :]
                        else:
                            t, blk, r0, rn = i % 2, u - 4, BD * (i // 2), BD
                            q, k = tr[:, 4 + blk, :], tr[:, 7 + blk, :]
                        w = P * (t + 1)
                        ins = pe.matmul(score_view(u, i), q[r0:r0 + rn, t * P:(t + 1) * P], k[r0:r0 + rn, 0:w],
                                        start=True, stop=True)
                    ins.then_inc(scores_ready, 1)

                def turn_probs(u):
                    U = UNITS * l + u
                    if u < 4:
                        pe.wait_ge(diff_ready, 4 * l + u + 1)
                    else:
                        pe.wait_ge(probs_ready, U + 1)
                    if U:
                        pe.wait_ge(turn_taken, U)
                    if u == 0:
                        pe.wait_ge(z_abs, l + 1)
                    if u == 1:
                        pe.wait_ge(decT_sb, l + 1)
                    for t in range(T):
                        if u < 4 and t != u % 2:
                            continue
                        for j in range(2):
                            src = s4[:, u % 2, 2 * j + (0 if u < 4 else t), :]
                            for kt in range(t + 1):
                                blk = j * (t + 1) + kt
                                ins = pe.transpose(ps[:, 2 + t, blk * P:(blk + 1) * P], src[:, kt * P:(kt + 1) * P], ident)
                    ins.then_inc(turn_ready, 1)

                def values(u):
                    pe.wait_ge(turn_taken, UNITS * l + u + 1)
                    if u == 4:
                        pe.wait_ge(oa_taken, l + 1)
                        pe.wait_ge(kv_act, KV_P * l + 3)
                    for t in range(T):
                        if u < 4 and t != u % 2:
                            continue
                        for j in range(2):
                            if u < 4:
                                hd = 2 * (u // 2) + j
                                o, v0 = ps[:, 0, t * S + AV * hd:t * S + AV * (hd + 1)], A_VAL + AV * hd
                            else:
                                hd = 2 * (u - 4) + j
                                o, v0 = ps[:, 1 - t, BD * hd:BD * (hd + 1)], B_VAL + BD * hd
                            for kt in range(t + 1):
                                ins = pe.matmul(o, pT[:, 2 * t + j * (t + 1) + kt, :], h[:, kt, v0:v0 + AV],
                                                start=(kt == 0), stop=(kt == t))
                    ins.then_inc(pv_done, 1)

                scores(0)
                piece(l, 0)
                for u in range(UNITS):
                    if u + 1 < UNITS:
                        scores(u + 1)
                    piece(l, u + 1, range(0, 6))
                    turn_probs(u)
                    piece(l, u + 1, range(6, KC))
                    values(u)
                    if u == 0:
                        pe.wait_ge(decay_ready, l + 1)
                        pe.wait_ge(acc_taken[3], acc_use(l, 5) // 2 + 1)
                        turn_heads(7, 3).then_inc(decT_psum, 1)

                pe.wait_ge(score_taken, 4 * UNITS * (l + 1))
                for s in range(GSTEPS):
                    if s:
                        pe.wait_ge(level_ready, (GSTEPS - 1) * l + s)
                    if s == 1:
                        pe.wait_ge(kv_act, KV_P * (l + 1))
                        pe.wait_ge(kv_dve, KV_P * (l + 1))
                    if s >= 2:
                        pe.wait_ge(level_taken, GSTEPS * l + s - 1)
                    for hp in range(2):
                        for pair in range(2):
                            for t in range(T if s <= LEVELS else 1):
                                r = slice(64 * hp, 64 * hp + 64)
                                if s == 0:
                                    q, k = tr[r, 10 + pair, :], tr[r, 12 + pair, :]
                                else:
                                    q, k = (qk[r, s % 2, n, pair * S:(pair + 1) * S] for n in range(2))
                                tq = t if s <= LEVELS else 1
                                at = (2 * pair + t if s <= LEVELS else pair) * P
                                ins = pe.matmul(ps[:, 4 + 2 * hp + s % 2, at:at + P], k[:, t * P:(t + 1) * P],
                                                q[:, tq * P:(tq + 1) * P], start=True, stop=True)
                    ins.then_inc(level_scores, 1)
                pe.wait_ge(level_taken, GSTEPS * (l + 1))
                for t in range(T):
                    for hd in range(CH):
                        pair, hp = divmod(hd, 2)
                        o = ps[:, 2 + t, CV * hd:CV * (hd + 1)]
                        v0 = C_VAL + CV * hd
                        ins = pe.matmul(o, st[:, hp, 2 * pair + t, :], h[:, t, v0:v0 + CV], start=True, stop=(t == 0))
                        if t == 1:
                            ins = pe.matmul(o, stx[:, hp, pair, :], h[:, 0, v0:v0 + CV], start=False, stop=True)
                ins.then_inc(gla_out, 1)

                for t in range(T):
                    turn_tile(TURN["k", l], k_mem, t)
                for t in range(T):
                    pe.wait_ge(mixed, T * l + t + 1)
                    turn_tile(TURN["mix", l], o_tok, t)
                for t in range(T):
                    turned(TURN["mix", l], t)
                    gemm_pair(l, IN_P + KV_P, t)

                q_p = IN_P + KV_P + OUT_P
                o_p = q_p + Q_P

                def turn_q(t):
                    pe.wait_ge((q_act, q_dve)[t], Q_P * (l + 1))
                    turn_tile(TURN["q", l], q_tok, t)

                def cross_scores(t):
                    turned(TURN["q", l], t)
                    for i in range(XH):
                        for c in range(2):
                            ins = pe.matmul(cross_bank(t, i), xT[:, 2 * i + c, t * P:(t + 1) * P], kT[:, 2 * i + c, :],
                                            start=(c == 0), stop=(c == 1))
                    ins.then_inc(xs_ready, 1)

                def cross_turn(t):
                    pe.wait_ge(xp_ready, T * l + t + 1)
                    for i in range(XH):
                        for kt in range(T):
                            blk = 2 * i + kt
                            ins = pe.transpose(ps[:, 4 + 2 * t + blk // 4, (blk % 4) * P:(blk % 4 + 1) * P],
                                               s4[:, t, i, kt * P:(kt + 1) * P], ident)
                    ins.then_inc(xturn_ready, 1)

                def cross_values(t):
                    pe.wait_ge(xturn_taken, T * l + t + 1)
                    for i in range(XH):
                        for kt in range(T):
                            ins = pe.matmul(ps[:, t + 2 * (i // 2), (i % 2) * XD:(i % 2 + 1) * XD], pT_cross[:, 2 * i + kt, :],
                                            v_mem[:, kt, i * XD:(i + 1) * XD], start=(kt == 0), stop=(kt == 1))
                    ins.then_inc(xo_ready, 1)

                def turn_xa(t):
                    pe.wait_ge(xo_taken, T * l + t + 1)
                    turn_tile(TURN["xa", l], o_xa, t)

                def turn_x(name, norm, t):
                    pe.wait_ge(ln_done, T * norm + t + 1)
                    turn_tile(TURN[name, l], x, t)

                turn_x("x1", 3 * l, 0)
                turned(TURN["x1", l], 0)
                gemm_pair(l, q_p, 0)
                turn_x("x1", 3 * l, 1)
                turn_q(0)
                turned(TURN["x1", l], 1)
                gemm(l, q_p, (1,))
                cross_scores(0)
                gemm(l, q_p + 1, (1,))
                cross_turn(0)
                turn_q(1)
                cross_values(0)
                cross_scores(1)
                turn_xa(0)
                turned(TURN["xa", l], 0)
                gemm(l, o_p, (0,))
                cross_turn(1)
                gemm(l, o_p + 1, (0,), range(KC // 2))
                cross_values(1)
                gemm(l, o_p + 1, (0,), range(KC // 2, KC))
                turn_xa(1)
                turned(TURN["xa", l], 1)
                gemm_pair(l, o_p, 1)
                turn_x("x2", 3 * l + 1, 0)
                turned(TURN["x2", l], 0)
                if l == 0:
                    def turn_chunk(m):
                        for t in range(T):
                            pe.wait_ge(hg_ready, 2 * m + t + 1)
                            if m >= 2:
                                pe.wait_ge(hT_sb[t], m - 1)
                            for c in range(min(4, F_DENSE // P - 4 * m)):
                                ins = pe.transpose(ps[:, 4 + 2 * (m % 2) + t, c * P:(c + 1) * P],
                                                   hg[:, m % 2, t, c * P:(c + 1) * P], ident)
                            ins.then_inc(hT_psum[t], 1)

                    for n in range(FFN_CHUNKS):
                        if n == 0:
                            gemm_pair(l, MIX_PANELS, 0)
                            turn_x("x2", 3 * l + 1, 1)
                            turned(TURN["x2", l], 1)
                            gemm_pair(l, MIX_PANELS, 1)
                        else:
                            gemm(l, MIX_PANELS + 2 * n)
                            gemm(l, MIX_PANELS + 2 * n + 1)
                        if n >= 1:
                            turn_chunk(n - 1)
                    def w2(i, t):
                        n, g = L1 - W2_P + i // 2, i % 2
                        if t == 0:
                            half_ready(l, n, g)
                        weights = (high_half(l, n, g), low_half(l, n, g))
                        for col in range(2):
                            for m, (p, q) in enumerate(HI_LO):
                                for c in range(2):
                                    k = 2 * i + c
                                    ins = pe.matmul(ps[:, t + 2 * col, :], (h_hi, h_lo)[p][:, k, t * P:(t + 1) * P],
                                                    weights[q][:, c, col * N:(col + 1) * N], start=(k == 0 and m == 0),
                                                    stop=(k == F_DENSE // P - 1 and m == 2))
                        return ins

                    last = F_DENSE // P // 2 - 1
                    by_tile = last + 1 - HIGH_SLOTS
                    for b in range(4):
                        pe.wait_ge(acc_taken[b], acc_use(l, MIX_PANELS + 2 * FFN_CHUNKS - 1) // 2 + 1)
                    for i in range(by_tile):
                        for t in range(T):
                            pe.wait_ge(hT_sb[t], i // 2 + 1)
                            ins = w2(i, t)
                            if i == 0 and t == 0:
                                turn_chunk(FFN_CHUNKS - 1)
                        ins.then_inc(dense_used, 1)
                    for t in range(T):
                        pe.wait_ge(hT_sb[t], FFN_CHUNKS)
                        for i in range(by_tile, last + 1):
                            ins = w2(i, t)
                            if i < last and t == 1:
                                ins.then_inc(dense_used, 1)
                        ins.then_inc(w2_ready, 1)
                    turn_x("x3", 3 * l + 2, 0)
                else:
                    turn_x("x2", 3 * l + 1, 1)
                    turned(TURN["x2", l], 1)

            for t in range(T):
                for k in range(KC):
                    ins = pe.matmul(ps[:, 4, t * NE:(t + 1) * NE], xT[:, k, t * P:(t + 1) * P], w_router[:, k, :],
                                    start=(k == 0), stop=(k == KC - 1))
            ins.then_inc(logit_psum, 1)
            pe.wait_ge(chosen_ready, 1)
            pe.matmul(ps[:, 5, 0:NE], before, chosen[:, 0, :], start=True, stop=True)
            pe.matmul(ps[:, 5, NE:2 * NE], before, chosen[:, 1, :], start=True, stop=False)
            pe.matmul(ps[:, 5, NE:2 * NE], ones, chosen[:, 0, :], start=False, stop=True)
            pe.matmul(ps[:, 5, 32:32 + NE], ones, chosen[:, 0, :], start=True, stop=False)
            pe.matmul(ps[:, 5, 32:32 + NE], ones, chosen[:, 1, :], start=False, stop=True).then_inc(rank2_psum, 1)

            def misc_bank(j, i):
                q = 2 + j
                b, uses = q % 2, q // 2
                if j >= 0:
                    pe.wait_ge(misc_taken[b], 7 * i + uses)
                return b

            def gather(i, j, count):
                pe.wait_ge(sel_ready, count)
                for g in range(2):
                    b = misc_bank(j + g, i)
                    for c in range(4):
                        for t in range(T):
                            k = 4 * g + c
                            ins = pe.matmul(ps[:, 6 + b, c * P:(c + 1) * P], x[:, t, k * P:(k + 1) * P], sel[:, t, :],
                                            start=(t == 0), stop=(t == T - 1))
                    ins.then_inc(misc_ready[b], 1)

            def turn_item(n, i, j):
                pe.wait_ge(he_ready, MOE_PAIRS * i + (n + 2))
                b = misc_bank(j, i)
                for c in range(4):
                    ins = pe.transpose(ps[:, 6 + b, c * P:(c + 1) * P], hge[:, n % 2, c * P:(c + 1) * P], ident)
                ins.then_inc(misc_ready[b], 1)

            gather(0, -2, 1)
            pe.sem_inc(half_used, SPLIT_SLOTS)

            def product(q, bank, x_hi, x_lo, c, cols, first, last):
                hi, lo = half_view(w_hi, q, SPLIT_SLOTS), half_view(w_lo, q, SPLIT_SLOTS)
                pe.matmul(ps[:, bank, :], x_hi, hi[:, c, cols], start=first, stop=False)
                pe.matmul(ps[:, bank, :], x_hi, lo[:, c, cols], start=False, stop=False)
                return pe.matmul(ps[:, bank, :], x_lo, hi[:, c, cols], start=False, stop=last)

            def scatter(i, part):
                t, n = divmod(part, 2)
                if part == 0:
                    pe.wait_ge(misc_taken[1], 7 * i + 6)
                    pe.wait_ge(y_act, i + 2)
                    pe.wait_ge(y_dve, i + 2)
                b = misc_bank(10 + part, i)
                pe.matmul(ps[:, 6 + b, :], gselT[:, t * P:(t + 1) * P], y[:, n * N:(n + 1) * N],
                          start=True, stop=True).then_inc(misc_ready[b], 1)

            def item(i, first=False):
                if first:
                    for b in range(2):
                        pe.wait_ge(misc_taken[b], 1)
                for q in range(4 * MOE_PAIRS):
                    n, g, r = q // 4, q // 2 % 2, q % 2
                    taken = (g_taken, he_ready)[g]
                    pe.wait_ge(lo_ready, ITEM_HALVES * i + (q + 1))
                    if r == 0 and n >= 2:
                        pe.wait_ge(taken, MOE_PAIRS * i + n)
                    elif r == 0 and n == 0:
                        pe.wait_ge(taken, MOE_PAIRS * i + 1)
                    for c in range(4):
                        k = 4 * r + c
                        ins = product(q, 2 * (n % 2) + g, xe_hi[:, k, :], xe_lo[:, k, :], c, slice(0, N),
                                      k == 0, k == KC - 1)
                    ins.then_inc(half_used, 1)
                    if q in SCATTERED_AT and not first:
                        scatter(i - 1, SCATTERED_AT.index(q))
                    if q % 4 == 3 and n >= 1:
                        turn_item(n - 1, i, n - 1)
                for q in range(4 * MOE_PAIRS, ITEM_HALVES):
                    jj, r = divmod(q - 4 * MOE_PAIRS, 2)
                    pe.wait_ge(lo_ready, ITEM_HALVES * i + (q + 1))
                    if q == 4 * MOE_PAIRS and first:
                        pe.wait_ge(table_ready, 1)
                    if q == 4 * MOE_PAIRS:
                        pe.wait_ge(y_act, i + 1)
                        pe.wait_ge(y_dve, i + 1)
                    if r == 0:
                        pe.wait_ge(misc_taken[jj % 2], 7 * i + (jj // 2 + 2))
                    for g in range(2):
                        for c in range(2):
                            k = 4 * jj + 2 * r + c
                            ins = product(q, 4 + g, he_hi[:, k, :], he_lo[:, k, :], c, slice(g * N, (g + 1) * N),
                                          k == 0, k == 4 * MOE_PAIRS - 1)
                    ins.then_inc(half_used, 1)
                    if q == 31:
                        turn_item(6, i, 6)
                    if q == 33:
                        gather(i, 7, i + 2)
                    if q == 37:
                        pe.wait_ge(gsel_ready, i + 1)
                        b = misc_bank(9, i)
                        for t in range(T):
                            ins = pe.transpose(ps[:, 6 + b, t * P:(t + 1) * P], gsel[:, t, :], ident)
                        ins.then_inc(misc_ready[b], 1)
                for b in range(2):
                    pe.wait_ge(misc_taken[b], 7 * i + (6 - b))

            item(0, first=True)
            n_items = pe.value_load(table_i[0:1, 0:1], min_val=NE, max_val=NE + EXTRA)
            last = pe.value_load(table_i[0:1, 4:5], min_val=NE - 1, max_val=NE + EXTRA - 1)
            with pe.Fori(1, n_items) as i:
                item(i)
            for part in range(2 * T):
                scatter(last, part)


_INS = ["x", "mem", "positions", "w_in", "lam_q1", "lam_k1", "lam_q2", "lam_k2", "diff_norm_g", "gla_wa2", "gla_ba",
        "gla_norm_g", "w_out", "ln_mix_g", "ln_mix_b", "xa_wq", "xa_wkv", "xa_wo", "ln_xa_g", "ln_xa_b",
        "ffd_w13", "ffd_w2", "moe_router", "moe_w13", "moe_w2", "ln_ffn_g", "ln_ffn_b"]


def kernel(**inputs):
    import concourse.bacc as bacc
    from concourse.bass_utils import run_bass_kernel_spmd as run

    nc = bacc.Bacc("TRN2", target_bir_lowering=False, num_devices=1)
    given = {name: np.ascontiguousarray(inputs[name]) for name in _INS}
    given.update(shape_constants())
    arrays, args = {}, {}
    for name, value in given.items():
        arrays[f"in_{name}_dram"] = value
        args[name] = nc.dram_tensor(f"in_{name}_dram", value.shape, mybir.dt.from_np(value.dtype),
                                    kind="ExternalInput").ap()
    result = nc.dram_tensor("out_0_dram", (1, S, D), F32, kind="ExternalOutput").ap()
    bass_decoder(nc, args, result)
    r = run(nc, [arrays], core_ids=[0])
    return r.results[0]["out_0_dram"]
```
